# Optimizing a Trainium2 kernel written in Bass

```python
import jax, jax.numpy as jnp
from jax import lax
import numpy as np
import math

D_MODEL = 1024
BATCH = 1
SEQ = 256
DEPTH = 1

SSM_WIDTH = D_MODEL // 2
SSM_GROUP = 16
SSM_GROUPS = SSM_WIDTH // SSM_GROUP
SSM_STATE = 64
NSA_HEADS = 8
NSA_KV_GROUPS = 2
HEADS_PER_GROUP = NSA_HEADS // NSA_KV_GROUPS
HEAD_DIM = 64
NSA_WIDTH = NSA_HEADS * HEAD_DIM
CMP_STRIDE = 16
CMP_BLOCK = 2 * CMP_STRIDE
CMP_HIDDEN = 2 * HEAD_DIM
SEL_BLOCK = 64
SEL_TOP_K = 16
WINDOW = 512
Q_BLOCK = 128
D_FF = 4 * D_MODEL
N_MIXERS = 2
KV_WIDTH = 3 * 2 * NSA_KV_GROUPS * HEAD_DIM
IN_WIDTH = SSM_WIDTH + NSA_WIDTH + KV_WIDTH + 3 * NSA_HEADS + N_MIXERS * D_MODEL
EPS = 1e-6
NEG_INF = -1e30
FORCE_BONUS = 1e4


def rmsnorm(x, g):
    xf = x.astype(jnp.float32)
    y = xf * lax.rsqrt(jnp.mean(xf * xf, axis=-1, keepdims=True) + EPS)
    return (y * g.astype(jnp.float32)).astype(x.dtype)

def masked_softmax(s, mask):
    s = jnp.where(mask, s.astype(jnp.float32), NEG_INF)
    p = jax.nn.softmax(s, axis=-1)
    return jnp.where(mask, p, 0.0)

def alibi_slopes():
    h = jnp.arange(1, NSA_HEADS + 1, dtype=jnp.float32)
    return jnp.exp2(-8.0 * h / NSA_HEADS).reshape(NSA_KV_GROUPS, HEADS_PER_GROUP, 1, 1)

def s5_mixer(u, a_re, a_im, log_dt, b_re, b_im, c_re, c_im, d_skip, w_glu, b_glu):
    bsz, s, _ = u.shape
    f32 = jnp.float32
    ug = u.astype(f32).reshape(bsz, s, SSM_GROUPS, SSM_GROUP)
    ar = a_re.astype(f32)
    ai = a_im.astype(f32)
    dt = jnp.exp(log_dt.astype(f32))[:, None]
    mag = jnp.exp(ar * dt)
    abar_re = mag * jnp.cos(ai * dt)
    abar_im = mag * jnp.sin(ai * dt)
    den = ar * ar + ai * ai
    nr = abar_re - 1.0
    fr = (nr * ar + abar_im * ai) / den
    fi = (abar_im * ar - nr * ai) / den
    br = b_re.astype(f32)
    bi = b_im.astype(f32)
    bbar_re = fr[..., None] * br - fi[..., None] * bi
    bbar_im = fr[..., None] * bi + fi[..., None] * br
    bu_re = jnp.einsum('bsgc,gpc->bsgp', ug, bbar_re)
    bu_im = jnp.einsum('bsgc,gpc->bsgp', ug, bbar_im)
    a_seq_re = jnp.broadcast_to(abar_re, (1, s, SSM_GROUPS, SSM_STATE))
    a_seq_im = jnp.broadcast_to(abar_im, (1, s, SSM_GROUPS, SSM_STATE))

    def combine(left, right):
        a1r, a1i, b1r, b1i = left
        a2r, a2i, b2r, b2i = right
        return (a2r * a1r - a2i * a1i, a2r * a1i + a2i * a1r,
                a2r * b1r - a2i * b1i + b2r, a2r * b1i + a2i * b1r + b2i)

    _, _, xr, xi = lax.associative_scan(combine, (a_seq_re, a_seq_im, bu_re, bu_im), axis=1)
    y = (jnp.einsum('bsgp,gcp->bsgc', xr, c_re.astype(f32))
         - jnp.einsum('bsgp,gcp->bsgc', xi, c_im.astype(f32))
         + d_skip.astype(f32).reshape(SSM_GROUPS, SSM_GROUP) * ug).reshape(bsz, s, SSM_WIDTH)
    yg = jax.nn.gelu(y)
    out = yg * jax.nn.sigmoid(yg @ w_glu.astype(f32) + b_glu.astype(f32))
    return out.astype(u.dtype)

def compress_blocks(tok, pe, w1, w2):
    bsz, g, s, d = tok.shape
    chunks = tok.reshape(bsz, g, s // CMP_STRIDE, CMP_STRIDE, d)
    blocks = jnp.concatenate([chunks[:, :, :-1], chunks[:, :, 1:]], axis=3) + pe
    flat = blocks.reshape(bsz, g, s // CMP_STRIDE - 1, CMP_BLOCK * d)
    return jax.nn.gelu(flat @ w1) @ w2

def nsa_mixer(q, kv, gate_logits, cmp_pe_k, cmp_pe_v, cmp_wk1, cmp_wk2, cmp_wv1, cmp_wv2,
              q_norm_g, k_norm_g):
    bsz, s, _ = q.shape
    G, HG, d = NSA_KV_GROUPS, HEADS_PER_GROUP, HEAD_DIM
    f32 = jnp.float32
    q = rmsnorm(q.reshape(bsz, s, G, HG, d), q_norm_g).transpose(0, 2, 3, 1, 4)
    kv = kv.reshape(bsz, s, 3, 2, G, d).transpose(2, 3, 0, 4, 1, 5)
    kc = rmsnorm(compress_blocks(kv[0, 0], cmp_pe_k, cmp_wk1, cmp_wk2), k_norm_g[0])
    vc = compress_blocks(kv[0, 1], cmp_pe_v, cmp_wv1, cmp_wv2)
    n_cmp = kc.shape[2]
    n_sel = s // SEL_BLOCK
    k_top = min(SEL_TOP_K, n_sel)
    ks = rmsnorm(kv[1, 0], k_norm_g[1]).reshape(bsz, G, n_sel, SEL_BLOCK, d)
    vs = kv[1, 1].reshape(bsz, G, n_sel, SEL_BLOCK, d)
    pad = ((0, 0), (0, 0), (WINDOW, 0), (0, 0))
    kw = jnp.pad(rmsnorm(kv[2, 0], k_norm_g[2]), pad)
    vw = jnp.pad(kv[2, 1], pad)
    gates = jax.nn.sigmoid(gate_logits.reshape(bsz, s, 3, G, HG).astype(f32))
    gates = gates.astype(q.dtype).transpose(0, 3, 4, 1, 2)
    slopes = alibi_slopes()
    scale = HEAD_DIM ** -0.5
    c_end = (jnp.arange(n_cmp) * CMP_STRIDE + CMP_BLOCK - 1).astype(f32)
    blk_ids = jnp.arange(n_sel)
    bi = jnp.arange(bsz)[:, None, None, None]
    gi = jnp.arange(G)[None, :, None, None]
    sel_off = jnp.arange(SEL_BLOCK)
    win_off = jnp.arange(Q_BLOCK + WINDOW)

    def query_block(i):
        qs = i * Q_BLOCK
        qb = lax.dynamic_slice_in_dim(q, qs, Q_BLOCK, axis=3)
        gb = lax.dynamic_slice_in_dim(gates, qs, Q_BLOCK, axis=3)
        t = qs + jnp.arange(Q_BLOCK)
        tf = t.astype(f32)
        dist_c = tf[:, None] - c_end[None, :]
        sc = jnp.einsum('bghqd,bgcd->bghqc', qb, kc).astype(f32) * scale - slopes * dist_c
        pc = masked_softmax(sc, dist_c >= 0)
        o_cmp = jnp.einsum('bghqc,bgcd->bghqd', pc.astype(vc.dtype), vc)
        imp = jnp.pad(pc.sum(axis=2), ((0, 0), (0, 0), (0, 0), (0, 1)))
        chunks = imp.reshape(bsz, G, Q_BLOCK, n_sel, SEL_BLOCK // CMP_STRIDE)
        prev = jnp.pad(chunks[..., :-1, -1], ((0, 0), (0, 0), (0, 0), (1, 0)))
        imp_sel = chunks.sum(axis=-1) + prev
        cur = t // SEL_BLOCK
        valid = blk_ids[None, :] <= cur[:, None]
        forced = ((blk_ids[None, :] == 0) | (blk_ids[None, :] == cur[:, None])
                  | (blk_ids[None, :] == cur[:, None] - 1))
        imp_sel = jnp.where(valid, imp_sel + jnp.where(forced, FORCE_BONUS, 0.0), NEG_INF)
        _, idx = lax.top_k(imp_sel, k_top)
        k_g = ks[bi, gi, idx].reshape(bsz, G, Q_BLOCK, k_top * SEL_BLOCK, d)
        v_g = vs[bi, gi, idx].reshape(bsz, G, Q_BLOCK, k_top * SEL_BLOCK, d)
        pos = (idx[..., None] * SEL_BLOCK + sel_off).reshape(bsz, G, Q_BLOCK, k_top * SEL_BLOCK)
        dist_s = (t[None, None, :, None] - pos).astype(f32)[:, :, None]
        ss = jnp.einsum('bghqd,bgqkd->bghqk', qb, k_g).astype(f32) * scale - slopes * dist_s
        ps = masked_softmax(ss, dist_s >= 0)
        o_slc = jnp.einsum('bghqk,bgqkd->bghqd', ps.astype(v_g.dtype), v_g)
        kwb = lax.dynamic_slice_in_dim(kw, qs, Q_BLOCK + WINDOW, axis=2)
        vwb = lax.dynamic_slice_in_dim(vw, qs, Q_BLOCK + WINDOW, axis=2)
        s_pos = qs - WINDOW + win_off
        dist_w = t[:, None] - s_pos[None, :]
        mask_w = (dist_w >= 0) & (dist_w < WINDOW) & (s_pos[None, :] >= 0)
        sw = jnp.einsum('bghqd,bgkd->bghqk', qb, kwb).astype(f32) * scale - slopes * dist_w.astype(f32)
        pw = masked_softmax(sw, mask_w)
        o_win = jnp.einsum('bghqk,bgkd->bghqd', pw.astype(vwb.dtype), vwb)
        return gb[..., 0:1] * o_cmp + gb[..., 1:2] * o_slc + gb[..., 2:3] * o_win

    out = lax.map(query_block, jnp.arange(s // Q_BLOCK))
    return out.transpose(1, 0, 4, 2, 3, 5).reshape(bsz, s, NSA_WIDTH)

def first_inputs(seed: int = 0) -> dict:
    key = jax.random.key(seed)
    ks = jax.random.split(key, 32)
    L = DEPTH
    f32 = jnp.float32

    def nrm(k, shape, scale):
        return jax.random.normal(k, shape, f32) * scale

    return {
        'x': nrm(ks[0], (BATCH, SEQ, D_MODEL), 1.0),
        'norm1_g': 1.0 + nrm(ks[1], (L, D_MODEL), 0.02),
        'w_in': nrm(ks[2], (L, D_MODEL, IN_WIDTH), D_MODEL ** -0.5),
        'ssm_a_re': -0.5 + nrm(ks[3], (L, SSM_GROUPS, SSM_STATE), 0.01),
        'ssm_a_im': np.pi * jnp.arange(SSM_STATE, dtype=f32) + nrm(ks[4], (L, SSM_GROUPS, SSM_STATE), 0.01),
        'ssm_log_dt': jax.random.uniform(ks[5], (L, SSM_GROUPS), f32, np.log(1e-3), np.log(1e-1)),
        'ssm_b_re': nrm(ks[6], (L, SSM_GROUPS, SSM_STATE, SSM_GROUP), (2 * SSM_GROUP) ** -0.5),
        'ssm_b_im': nrm(ks[7], (L, SSM_GROUPS, SSM_STATE, SSM_GROUP), (2 * SSM_GROUP) ** -0.5),
        'ssm_c_re': nrm(ks[8], (L, SSM_GROUPS, SSM_GROUP, SSM_STATE), SSM_STATE ** -0.5),
        'ssm_c_im': nrm(ks[9], (L, SSM_GROUPS, SSM_GROUP, SSM_STATE), SSM_STATE ** -0.5),
        'ssm_d': nrm(ks[10], (L, SSM_WIDTH), 1.0),
        'ssm_w_glu': nrm(ks[11], (L, SSM_WIDTH, SSM_WIDTH), SSM_WIDTH ** -0.5),
        'ssm_b_glu': nrm(ks[12], (L, SSM_WIDTH), 0.01),
        'cmp_pe_k': nrm(ks[13], (L, CMP_BLOCK, HEAD_DIM), 0.1),
        'cmp_pe_v': nrm(ks[14], (L, CMP_BLOCK, HEAD_DIM), 0.1),
        'cmp_wk1': nrm(ks[15], (L, CMP_BLOCK * HEAD_DIM, CMP_HIDDEN), (CMP_BLOCK * HEAD_DIM) ** -0.5),
        'cmp_wk2': nrm(ks[16], (L, CMP_HIDDEN, HEAD_DIM), CMP_HIDDEN ** -0.5),
        'cmp_wv1': nrm(ks[17], (L, CMP_BLOCK * HEAD_DIM, CMP_HIDDEN), (CMP_BLOCK * HEAD_DIM) ** -0.5),
        'cmp_wv2': nrm(ks[18], (L, CMP_HIDDEN, HEAD_DIM), CMP_HIDDEN ** -0.5),
        'q_norm_g': 1.0 + nrm(ks[19], (L, HEAD_DIM), 0.02),
        'k_norm_g': 1.0 + nrm(ks[20], (L, 3, HEAD_DIM), 0.02),
        'w_proj_ssm': nrm(ks[21], (L, SSM_WIDTH, D_MODEL), SSM_WIDTH ** -0.5),
        'w_proj_nsa': nrm(ks[22], (L, NSA_WIDTH, D_MODEL), NSA_WIDTH ** -0.5),
        'w_out': nrm(ks[23], (L, D_MODEL, D_MODEL), D_MODEL ** -0.5),
        'norm2_g': 1.0 + nrm(ks[24], (L, D_MODEL), 0.02),
        'w_up': nrm(ks[25], (L, D_MODEL, D_FF), D_MODEL ** -0.5),
        'w_down': nrm(ks[26], (L, D_FF, D_MODEL), D_FF ** -0.5),
    }

def first_block(x, norm1_g, w_in, ssm_a_re, ssm_a_im, ssm_log_dt, ssm_b_re, ssm_b_im, ssm_c_re, ssm_c_im,
              ssm_d, ssm_w_glu, ssm_b_glu, cmp_pe_k, cmp_pe_v, cmp_wk1, cmp_wk2, cmp_wv1, cmp_wv2,
              q_norm_g, k_norm_g, w_proj_ssm, w_proj_nsa, w_out, norm2_g, w_up, w_down):
    bsz, s, _ = x.shape
    o1 = SSM_WIDTH
    o2 = o1 + NSA_WIDTH
    o3 = o2 + KV_WIDTH
    o4 = o3 + 3 * NSA_HEADS
    for l in range(DEPTH):
        h = rmsnorm(x, norm1_g[l])
        hp = h @ w_in[l]
        y_ssm = s5_mixer(hp[..., :o1], ssm_a_re[l], ssm_a_im[l], ssm_log_dt[l], ssm_b_re[l], ssm_b_im[l],
                         ssm_c_re[l], ssm_c_im[l], ssm_d[l], ssm_w_glu[l], ssm_b_glu[l])
        y_nsa = nsa_mixer(hp[..., o1:o2], hp[..., o2:o3], hp[..., o3:o4], cmp_pe_k[l], cmp_pe_v[l],
                          cmp_wk1[l], cmp_wk2[l], cmp_wv1[l], cmp_wv2[l], q_norm_g[l], k_norm_g[l])
        gate = jax.nn.sigmoid(hp[..., o4:].reshape(bsz, s, N_MIXERS, D_MODEL))
        merged = gate[..., 0, :] * (y_ssm @ w_proj_ssm[l]) + gate[..., 1, :] * (y_nsa @ w_proj_nsa[l])
        x = x + merged @ w_out[l]
        h2 = rmsnorm(x, norm2_g[l])
        x = x + jnp.square(jax.nn.relu(h2 @ w_up[l])) @ w_down[l]
    return x


DEPTH_2 = 2

N_RET_LAYERS = (DEPTH_2 + 1) // 2
N_MLA_LAYERS = DEPTH_2 // 2
MIX_WIDTH = D_MODEL
MEM_LEN = 256
MEM_HEADS = 4
MEM_HEAD_DIM = 64
MEM_WIDTH = MEM_HEADS * MEM_HEAD_DIM
TOK_WIDTH = MIX_WIDTH - MEM_WIDTH
RET_HEADS = 6
RET_DK = 128
RET_DV = TOK_WIDTH // RET_HEADS
RET_CHUNK = 128
RET_IN = 4 * TOK_WIDTH + MEM_WIDTH
MLA_HEADS = 6
MLA_NOPE = 64
MLA_ROPE = 32
MLA_DV = TOK_WIDTH // MLA_HEADS
MLA_Q_RANK = 256
MLA_KV_RANK = 128
MLA_IN = MLA_Q_RANK + MLA_KV_RANK + MLA_ROPE + MEM_WIDTH
MLA_SCALE = (MLA_NOPE + MLA_ROPE) ** -0.5
D_FF_2 = 2816
FFN_RES_WEIGHT = 0.5
ROPE_THETA = 10000.0
NORM_EPS = 1e-6


def rms_norm(x, g):
    xf = x.astype(jnp.float32)
    y = xf * lax.rsqrt(jnp.mean(xf * xf, axis=-1, keepdims=True) + NORM_EPS)
    return (y * g.astype(jnp.float32)).astype(x.dtype)

def head_layer_norm(y, g):
    mu = jnp.mean(y, axis=-1, keepdims=True)
    var = jnp.mean(jnp.square(y - mu), axis=-1, keepdims=True)
    return (y - mu) * lax.rsqrt(var + NORM_EPS) * g.astype(jnp.float32)

def rope_tables(positions, dim):
    inv = 1.0 / (ROPE_THETA ** (jnp.arange(0, dim, 2, dtype=jnp.float32) / dim))
    ang = positions.astype(jnp.float32)[..., None] * inv
    return jnp.cos(ang), jnp.sin(ang)

def apply_rope(x, cos, sin):
    half = x.shape[-1] // 2
    x1, x2 = x[..., :half], x[..., half:]
    c = cos[:, :, None, :].astype(x.dtype)
    s = sin[:, :, None, :].astype(x.dtype)
    return jnp.concatenate([x1 * c - x2 * s, x1 * s + x2 * c], axis=-1)

def swiglu(h, w_gu, w_down):
    g, u = jnp.split(h @ w_gu, 2, axis=-1)
    return (jax.nn.silu(g) * u) @ w_down

def retention_chunkwise(q, k, v, log_gamma, strict):
    B, S, H, dk = q.shape
    dv = v.shape[-1]
    n = S // RET_CHUNK
    C = RET_CHUNK
    q = q.astype(jnp.float32).reshape(B, n, C, H, dk)
    k = k.astype(jnp.float32).reshape(B, n, C, H, dk)
    v = v.astype(jnp.float32).reshape(B, n, C, H, dv)
    lg = log_gamma.astype(jnp.float32)
    idx = jnp.arange(C, dtype=jnp.float32)
    diff = idx[:, None] - idx[None, :]
    mask = diff > 0 if strict else diff >= 0
    decay = jnp.where(mask[None], jnp.exp(jnp.where(mask, diff, 0.0)[None] * lg[:, None, None]), 0.0)
    scores = jnp.einsum('bnihd,bnjhd->bnhij', q, k) * decay[None, None]
    intra = jnp.einsum('bnhij,bnjhv->bnihv', scores, v)
    k_w = k * jnp.exp((C - 1.0 - idx)[:, None] * lg[None, :])[None, None, :, :, None]
    chunk_kv = jnp.einsum('bnjhd,bnjhv->bnhdv', k_w, v)
    g_chunk = jnp.exp(C * lg)[None, :, None, None]

    def step(state, kv_n):
        return state * g_chunk + kv_n, state

    init = jnp.zeros((B, H, dk, dv), jnp.float32)
    _, states = lax.scan(step, init, jnp.moveaxis(chunk_kv, 1, 0))
    states = jnp.moveaxis(states, 0, 1)
    q_w = q * jnp.exp((idx + 1.0)[:, None] * lg[None, :])[None, None, :, :, None]
    cross = jnp.einsum('bnihd,bnhdv->bnihv', q_w, states)
    return (intra + cross).reshape(B, S, H, dv)

def retention_mixer(h, w_in, log_decay, head_norm, cos, sin):
    B, S, _ = h.shape
    T = TOK_WIDTH
    q, k, v, g, qm = jnp.split(h @ w_in, [T, 2 * T, 3 * T, 4 * T], axis=-1)
    q = apply_rope(q.reshape(B, S, RET_HEADS, RET_DK), cos, sin)
    k = apply_rope(k.reshape(B, S, RET_HEADS, RET_DK), cos, sin) * (RET_DK ** -0.5)
    v = v.reshape(B, S, RET_HEADS, RET_DV)
    y_fwd = retention_chunkwise(q, k, v, log_decay[0], strict=False)
    y_bwd = retention_chunkwise(q[:, ::-1], k[:, ::-1], v[:, ::-1], log_decay[1], strict=True)[:, ::-1]
    y = head_layer_norm(y_fwd + y_bwd, head_norm).reshape(B, S, T).astype(h.dtype)
    return jax.nn.silu(g) * y, qm

def dense_attention_blocked(q, k, v, scale):
    B, S, H, dq = q.shape
    dv = v.shape[-1]
    n = S // Q_BLOCK
    qb = q.reshape(B, n, Q_BLOCK, H, dq).transpose(1, 0, 2, 3, 4)

    def one_block(q_blk):
        s = jnp.einsum('bqhd,bkhd->bhqk', q_blk, k).astype(jnp.float32) * scale
        p = jax.nn.softmax(s, axis=-1).astype(v.dtype)
        return jnp.einsum('bhqk,bkhv->bqhv', p, v)

    o = lax.map(one_block, qb)
    return o.transpose(1, 0, 2, 3, 4).reshape(B, S, H * dv)

def mla_mixer(h, w_in, q_norm, kv_norm, w_uq, w_ukv, cos, sin):
    B, S, _ = h.shape
    c_q, c_kv, k_r, qm = jnp.split(
        h @ w_in, [MLA_Q_RANK, MLA_Q_RANK + MLA_KV_RANK, MLA_Q_RANK + MLA_KV_RANK + MLA_ROPE], axis=-1)
    c_q = rms_norm(c_q, q_norm)
    c_kv = rms_norm(c_kv, kv_norm)
    q = (c_q @ w_uq).reshape(B, S, MLA_HEADS, MLA_NOPE + MLA_ROPE)
    q = jnp.concatenate([q[..., :MLA_NOPE], apply_rope(q[..., MLA_NOPE:], cos, sin)], axis=-1)
    kv = (c_kv @ w_ukv).reshape(B, S, MLA_HEADS, MLA_NOPE + MLA_DV)
    k_nope, v = kv[..., :MLA_NOPE], kv[..., MLA_NOPE:]
    k_rope = apply_rope(k_r.reshape(B, S, 1, MLA_ROPE), cos, sin)
    k = jnp.concatenate([k_nope, jnp.broadcast_to(k_rope, (B, S, MLA_HEADS, MLA_ROPE))], axis=-1)
    return dense_attention_blocked(q, k, v, MLA_SCALE), qm

def memory_attention(qm, mem_n, w_kv):
    B, S, _ = qm.shape
    L = mem_n.shape[1]
    q = qm.reshape(B, S, MEM_HEADS, MEM_HEAD_DIM)
    mk, mv = jnp.split(mem_n @ w_kv, 2, axis=-1)
    mk = mk.reshape(B, L, MEM_HEADS, MEM_HEAD_DIM)
    mv = mv.reshape(B, L, MEM_HEADS, MEM_HEAD_DIM)
    s = jnp.einsum('bshd,bmhd->bhsm', q, mk).astype(jnp.float32) * (MEM_HEAD_DIM ** -0.5)
    p = jax.nn.softmax(s, axis=-1).astype(mv.dtype)
    return jnp.einsum('bhsm,bmhd->bshd', p, mv).reshape(B, S, MEM_WIDTH)

def second_inputs(seed: int = 0) -> dict:
    key = jax.random.key(seed)
    ks = jax.random.split(key, 17)
    f32 = jnp.float32

    def w(k, shape, fan_in):
        return jax.random.normal(k, shape, f32) * (fan_in ** -0.5)

    def gain(k, shape):
        return 1.0 + 0.02 * jax.random.normal(k, shape, f32)

    x = jax.random.normal(ks[0], (BATCH, SEQ, D_MODEL), f32)
    mem = jax.random.normal(ks[1], (BATCH, MEM_LEN, D_MODEL), f32)
    offsets = jax.random.randint(ks[2], (BATCH, 1), 0, 1024, dtype=jnp.int32)
    positions = (offsets + jnp.arange(SEQ, dtype=jnp.int32)[None, :]).astype(jnp.int32)
    base_decay = jnp.log(1.0 - 2.0 ** (-5.0 - jnp.arange(RET_HEADS, dtype=f32)))
    ret_log_decay = base_decay[None, None, :] * (1.0 + 0.05 * jax.random.normal(ks[10], (N_RET_LAYERS, 2, RET_HEADS), f32))
    return {
        "x": x,
        "mem": mem,
        "positions": positions,
        "norm_gains": gain(ks[3], (DEPTH_2, 6, D_MODEL)),
        "ffn_w_gu": w(ks[4], (DEPTH_2, 2, D_MODEL, 2 * D_FF_2), D_MODEL),
        "ffn_w_down": w(ks[5], (DEPTH_2, 2, D_FF_2, D_MODEL), D_FF_2),
        "w_o": w(ks[6], (DEPTH_2, MIX_WIDTH, D_MODEL), MIX_WIDTH),
        "mem_norm": gain(ks[7], (D_MODEL,)),
        "mem_w_kv": w(ks[8], (DEPTH_2, D_MODEL, 2 * MEM_WIDTH), D_MODEL),
        "ret_w_in": w(ks[9], (N_RET_LAYERS, D_MODEL, RET_IN), D_MODEL),
        "ret_log_decay": ret_log_decay,
        "ret_head_norm": gain(ks[11], (N_RET_LAYERS, RET_HEADS, RET_DV)),
        "mla_w_in": w(ks[12], (N_MLA_LAYERS, D_MODEL, MLA_IN), D_MODEL),
        "mla_q_norm": gain(ks[13], (N_MLA_LAYERS, MLA_Q_RANK)),
        "mla_kv_norm": gain(ks[14], (N_MLA_LAYERS, MLA_KV_RANK)),
        "mla_w_uq": w(ks[15], (N_MLA_LAYERS, MLA_Q_RANK, MLA_HEADS * (MLA_NOPE + MLA_ROPE)), MLA_Q_RANK),
        "mla_w_ukv": w(ks[16], (N_MLA_LAYERS, MLA_KV_RANK, MLA_HEADS * (MLA_NOPE + MLA_DV)), MLA_KV_RANK),
    }

def second_block(x, mem, positions, norm_gains, ffn_w_gu, ffn_w_down, w_o, mem_norm, mem_w_kv,
              ret_w_in, ret_log_decay, ret_head_norm,
              mla_w_in, mla_q_norm, mla_kv_norm, mla_w_uq, mla_w_ukv):
    cos_ret, sin_ret = rope_tables(positions, RET_DK)
    cos_mla, sin_mla = rope_tables(positions, MLA_ROPE)
    mem_n = rms_norm(mem, mem_norm)

    for l in range(DEPTH_2):
        ng = norm_gains[l]
        x = x + FFN_RES_WEIGHT * rms_norm(swiglu(rms_norm(x, ng[0]), ffn_w_gu[l, 0], ffn_w_down[l, 0]), ng[1])
        h = rms_norm(x, ng[2])
        r = l // N_MIXERS
        if l % N_MIXERS == 0:
            tok, qm = retention_mixer(h, ret_w_in[r], ret_log_decay[r], ret_head_norm[r], cos_ret, sin_ret)
        else:
            tok, qm = mla_mixer(h, mla_w_in[r], mla_q_norm[r], mla_kv_norm[r], mla_w_uq[r], mla_w_ukv[r],
                                cos_mla, sin_mla)
        mem_out = memory_attention(qm, mem_n, mem_w_kv[l])
        mix = jnp.concatenate([tok, mem_out], axis=-1) @ w_o[l]
        x = x + rms_norm(mix, ng[3])
        x = x + FFN_RES_WEIGHT * rms_norm(swiglu(rms_norm(x, ng[4]), ffn_w_gu[l, 1], ffn_w_down[l, 1]), ng[5])
    return x


def setup_inputs(seed=0):
    out = dict(first_inputs(seed))
    for name, value in second_inputs(seed + 1).items():
        if name != "x":
            out[name + "_2"] = value
    return out


def reference(
    x, norm1_g, w_in, ssm_a_re, ssm_a_im, ssm_log_dt, ssm_b_re, ssm_b_im, ssm_c_re, ssm_c_im,
    ssm_d, ssm_w_glu, ssm_b_glu, cmp_pe_k, cmp_pe_v, cmp_wk1, cmp_wk2, cmp_wv1, cmp_wv2,
    q_norm_g, k_norm_g, w_proj_ssm, w_proj_nsa, w_out, norm2_g, w_up, w_down, mem_2,
    positions_2, norm_gains_2, ffn_w_gu_2, ffn_w_down_2, w_o_2, mem_norm_2, mem_w_kv_2,
    ret_w_in_2, ret_log_decay_2, ret_head_norm_2, mla_w_in_2, mla_q_norm_2, mla_kv_norm_2,
    mla_w_uq_2, mla_w_ukv_2,
):
    x = first_block(
        x, norm1_g, w_in, ssm_a_re, ssm_a_im, ssm_log_dt, ssm_b_re, ssm_b_im, ssm_c_re,
        ssm_c_im, ssm_d, ssm_w_glu, ssm_b_glu, cmp_pe_k, cmp_pe_v, cmp_wk1, cmp_wk2, cmp_wv1,
        cmp_wv2, q_norm_g, k_norm_g, w_proj_ssm, w_proj_nsa, w_out, norm2_g, w_up, w_down,
    )
    return second_block(
        x, mem_2, positions_2, norm_gains_2, ffn_w_gu_2, ffn_w_down_2, w_o_2, mem_norm_2,
        mem_w_kv_2, ret_w_in_2, ret_log_decay_2, ret_head_norm_2, mla_w_in_2, mla_q_norm_2,
        mla_kv_norm_2, mla_w_uq_2, mla_w_ukv_2,
    )


_drawn_inputs = setup_inputs


def setup_inputs(seed=0):
    import zlib

    import numpy as np

    out = dict(_drawn_inputs(seed))
    spreads = {}
    factors = {'norm1_g': 4.948,
     'ssm_a_re': 200.0,
     'ssm_b_re': 3.183,
     'ssm_b_im': 3.204,
     'ssm_c_re': 3.229,
     'ssm_c_im': 3.231,
     'ssm_b_glu': 26.531,
     'cmp_pe_k': 8.0,
     'q_norm_g': 8.0,
     'k_norm_g': 8.0,
     'mem_norm_2': 64.0,
     'ret_head_norm_2': 200.0,
     'mla_q_norm_2': 62.401,
     'mla_kv_norm_2': 52.096,
     'cmp_pe_v': 3.073,
     'norm2_g': 3.197,
     'norm_gains_2': 5.163,
     'ret_log_decay_2': 2.906}
    for name, (base, spread) in spreads.items():
        noise = np.random.default_rng([zlib.crc32(name.encode()), seed]).standard_normal(out[name].shape)
        drawn = base * np.exp(spread * noise) if base else spread * noise
        out[name] = __import__('jax').numpy.asarray(drawn.astype(out[name].dtype))
    for name, factor in factors.items():
        out[name] = (out[name] * factor).astype(out[name].dtype)
    return out
```

```python
import concourse.bass as bass
from concourse import mybir
from concourse.alu_op_type import AluOpType as ALU
from contextlib import ExitStack
import numpy as np

F32 = mybir.dt.float32
F32R = mybir.dt.float32r
ACT = mybir.ActivationFunctionType
AX = mybir.AxisListType.X

P = 128
T = 256
TT = T // P
D = 1024
KT = D // P
UNIT = 2048
RAW = 4
SPL = 2
EPS = 1e-6
NEG = -1e30
MAGIC = 1.5 * 2.0 ** 23
C_HI, C_LO = 6.28125, 2.0 * np.pi - 6.28125
TWO_PI_IN = 6.283185

SSM_W, GLU_KT = 512, 4
N_STATE_TILES = 16
NH, NG, HG, DH = 8, 2, 4, 64
N_CMP, CMP_STRIDE, CMP_BLOCK = 15, 16, 32
BLOCK_COLS = N_CMP * CMP_STRIDE
FF1_T, FF2_T = 4096 // P, 2816 // P
RH, MH, XH = 6, 4, 6
NOPE, ROPE = 64, 32

VECS = [("norm1", 8), ("norm2", 8), ("ng", 96), ("memg", 8), ("a_re", 16), ("a_im", 16), ("log_dt", 16),
        ("d_skip", 4), ("b_glu", 4), ("qg", 1), ("kg", 3), ("head_norm", 6), ("cq_g", 2), ("ckv_g", 1),
        ("lg_f", 6), ("lg_b", 6), ("inv_ret", 1), ("inv_mla", 1), ("half_pi", 1), ("eps", 1)]
VOFF, _o = {}, 0
for _n, _c in VECS:
    VOFF[_n] = (_o, _o + _c)
    _o += _c
NVEC = _o

TABS = [("ident", 128), ("ones", 128), ("bones", 128), ("gsel", 2), ("rot_ret", 128), ("rot_mla", 128), ("tok", 256)]
TOFF, _o = {}, 0
for _n, _c in TABS:
    TOFF[_n] = (_o, _o + _c)
    _o += _c
NTAB = _o


def unit_list():
    out = []

    def add(name, first, n, cols=UNIT, split=True):
        for c in range(first, first + n):
            out.append((name, c, cols, split))
    add("w_u", 0, 2)
    add("w_q", 0, 2)
    add("w_kv", 1, 2)
    add("w_kv", 0, 1)
    add("w_mg", 0, 8, split=False)
    add("w_mem", 0, 4, split=False)
    add("w_c1", 0, 2, split=False)
    add("w_glu", 0, 2, 1024)
    add("w_ps", 0, 4, 1024)
    add("w_pn", 0, 4, 1024)
    add("w_out", 0, 4)
    add("w_up", 0, 16)
    add("w_dn", 0, 16)
    for l in range(2):
        add("w_gu", l * 44, 22)
        add("w_fd", l * 32, 16, 11 * P)
        if l == 0:
            add("w_ret", 0, 13)
        else:
            add("w_mla", 0, 3)
        add("w_o", l * 4, 4)
        add("w_gu", l * 44 + 22, 22)
        add("w_fd", l * 32 + 16, 16, 11 * P)
    return out


UNITS = unit_list()
NU = len(UNITS)
SPLIT_BEFORE = [sum(u[3] for u in UNITS[:n]) for n in range(NU + 1)]
PLAIN_BEFORE = [n - s for n, s in enumerate(SPLIT_BEFORE)]
SPLITS = [n for n, u in enumerate(UNITS) if u[3]]
AT = {(u[0], u[1]): n for n, u in enumerate(UNITS)}
NOT_GROUP = ("w_dn", "w_fd", "w_c1")
GROUP = [sum(u[0] not in NOT_GROUP for u in UNITS[:n]) for n in range(NU + 1)]


class Chain:

    def __init__(self, eng, sem):
        self.eng, self.sem, self.n, self.i, self.per = eng, sem, 0, None, 0

    def __call__(self, ins):
        self.n += 1
        ins.then_inc(self.sem, 1)
        self.eng.wait_ge(self.sem, self.n if self.i is None else self.i * self.per + self.n)

    def open(self, i, per):
        self.i, self.per, self.at = i, per, self.n

    def close(self, rounds):
        assert self.n - self.at == self.per, (self.n - self.at, self.per)
        self.n = self.at + self.per * rounds
        self.i = None


def at_round(base, i, step):
    return base if i is None else i * step + base


def attention_plan(QK, rq, alibi, alibc, maskc, gate, kcr, VV, VC, qmT, mkT, mv, rqT, rkT, rv, mixf, ynf, pTs):
    subs, parts = [], {}

    def sub(**k):
        k["index"] = len(subs)
        subs.append(k)
        return k

    npv = 0
    steps = []
    for qt in range(TT):
        for g in range(NG):
            rows, qs, nkt = slice(g * DH, g * DH + DH), slice(qt * P, qt * P + P), qt + 1
            for b in range(2):
                steps.append(("sub", sub(
                    nh=HG, nk=nkt * P, base=8 * b, kts=nkt, pv=npv,
                    q=[QK[rows, h, qs] for h in range(HG)], k=[QK[rows, 4 + b, 0:nkt * P]] * HG,
                    rowscale=[rq[:, qt, h, g:g + 1] for h in range(HG)],
                    bias=[alibi[:, g * HG + h, (TT - nkt) * P:T] for h in range(HG)],
                    gate=gate[:, qt, (b + 1) * NH + g * HG:(b + 1) * NH + g * HG + HG], mask=None, scale=None)))
            steps.append(("sub", sub(
                nh=HG, nk=N_CMP, base=16, kts=0, pv=npv,
                q=[QK[rows, h, qs] for h in range(HG)], k=[kcr[rows, 3, 0:N_CMP]] * HG,
                rowscale=[rq[:, qt, h, g:g + 1] for h in range(HG)],
                bias=[alibc[:, qt, g * HG + h, 0:N_CMP] for h in range(HG)],
                gate=gate[:, qt, g * HG:g * HG + HG], mask=maskc[:, qt, :, 0:N_CMP], scale=None)))
            outs = []
            for h in range(HG):
                terms = [(VV[:, b, kt, rows], pTs[:, 8 * b + h * nkt + kt, :]) for b in range(2) for kt in range(nkt)]
                terms.append((VC[:, h, rows], pTs[:, 16, :]))
                outs.append((rows, h, terms))
            steps.append(("pv", dict(index=npv, outs=outs, rows=rows, n=HG, dest=ynf[rows, :, qs])))
            npv += 1
    parts["nsa"] = steps
    for part in ("mem0", "mla", "mem1"):
        steps = []
        for qt in range(TT):
            qs = slice(qt * P, qt * P + P)
            if part == "mla":
                for half in range(2):
                    hs = range(3 * half, 3 * half + 3)
                    steps.append(("sub", sub(
                        nh=3, nk=T, base=8 * (npv % 2), kts=TT, pv=npv - 1,
                        q=[rqT[0:96, h, qs] for h in hs], k=[rkT[0:96, h, :] for h in hs],
                        rowscale=None, bias=None, gate=None, mask=None, scale=float((NOPE + ROPE) ** -0.5))))
                    outs = [(slice(0, P), i, [(rv[:, kt, h * P:h * P + P], pTs[:, 8 * (npv % 2) + i * TT + kt, :])
                                              for kt in range(TT)]) for i, h in enumerate(hs)]
                    steps.append(("pv", dict(index=npv, outs=outs, rows=slice(0, P), n=3,
                                             dest=mixf[:, 3 * half:3 * half + 3, qs])))
                    npv += 1
            else:
                l = int(part[3])
                order = (0, 2, 1, 3)
                steps.append(("sub", sub(
                    nh=MH, nk=T, base=8 * (npv % 2), kts=TT, pv=npv - 1,
                    q=[qmT[h % 2 * DH:h % 2 * DH + DH, h // 2, qs] for h in order],
                    k=[mkT[h % 2 * DH:h % 2 * DH + DH, l, h // 2, :] for h in order],
                    rowscale=None, bias=None, gate=None, mask=None, scale=float(DH ** -0.5))))
                outs = [(slice(h % 2 * DH, h % 2 * DH + DH), h // 2,
                         [(mv[:, l, kt, h * DH:h * DH + DH], pTs[:, 8 * (npv % 2) + i * TT + kt, :])
                          for kt in range(TT)]) for i, h in enumerate(order)]
                steps.append(("pv", dict(index=npv, outs=outs, rows=slice(0, P), n=2, dest=mixf[:, RH:RH + 2, qs])))
                npv += 1
        parts[part] = steps
    chunk = 0
    for s in subs:
        tiles = [(h, kt) for h in range(s["nh"]) for kt in range(s["kts"])] or [None]
        s["hs"] = {T: T, P: P, N_CMP: 16}[s["nk"]]
        s["chunks"] = [tiles[c:c + 4] for c in range(0, len(tiles), 4)]
        s["chunk0"] = chunk
        chunk += len(s["chunks"])
    exp_to, reads, cmps = [0], 0, []
    for s in subs:
        exp_to.append(exp_to[-1] + s["nh"])
        if s["bias"]:
            reads += 1
        s["read"] = reads
        if s["mask"] is not None:
            s["cmp"] = len(cmps)
            s["pc_free"] = cmps[-2] if len(cmps) >= 2 else 0
            cmps.append(s["chunk0"] + len(s["chunks"]))
    parts_out, copied = {}, 0
    for name, steps in parts.items():
        for what, s in steps:
            if what == "sub":
                copied = s["chunk0"] + len(s["chunks"])
            else:
                s["copied"] = copied
                parts_out[name] = s["index"] + 1
    return subs, parts, exp_to, parts_out


def program(nc, A, out):
    ctx = ExitStack()
    with ctx:
        sems = {}

        def S(name):
            if name not in sems:
                sems[name] = ctx.enter_context(nc.semaphore(name))
            return sems[name]

        base = [nc.sbuf_base + (-nc.sbuf_base) % 64]

        def sb(name, shape, dt=F32, where=base):
            t = nc.alloc_sbuf_tensor_at(name, shape, dt, offset=where[0])
            size = 4 * int(np.prod(shape[1:]))
            where[0] += size + (-size) % 64
            return t

        raw = sb("raw", [P, RAW, UNIT])
        whi = sb("whi", [P, SPL, UNIT], F32R)
        wlo = sb("wlo", [P, SPL, UNIT], F32R)
        xT = sb("xT", [P, KT, T])
        at_xg = [base[0]]
        xg = sb("xg", [P, KT, T])
        at_ahi = [base[0]]
        ahi = sb("ahi", [P, KT, T], F32R)
        at_alo = [base[0]]
        alo = sb("alo", [P, KT, T], F32R)
        at_yT = [base[0]]
        yT = sb("yT", [P, KT, T])
        at_sq = [base[0]]
        sq = sb("sq", [P, 2, T])
        acc = sb("acc", [P, T])
        acc2 = sb("acc2", [P, 2, T])
        half_q = sb("half_q", [P, 1])
        warm = sb("warm", [P, 1])
        sd = sb("sd", [P, T + TT])
        r = sb("r", [P, T + TT])
        rm = sb("rm", [P, T + TT])
        vecs = sb("vecs", [P, NVEC])
        tabs = sb("tabs", [P, NTAB])
        half_g = sb("half_g", [P, 96])
        mkT = sb("mkT", [P, 2, 2, T])
        mv = sb("mv", [P, 2, TT, T])
        amx = sb("amx", [P, 2, 3, 4])
        V = {n: vecs[:, a:b] for n, (a, b) in VOFF.items()}
        C = {n: tabs[:, a:b] for n, (a, b) in TOFF.items()}
        sS = sb("sS", [P, 2, 4 * T], where=[at_yT[0]])
        pP = sb("pP", [P, 2, 4 * T], where=[at_xg[0]])
        phase = base[0]

        w = [phase]
        at_uT = [w[0]]
        uT = sb("uT", [P, 4, T], where=w)
        ynf = sb("ynf", [P, 4, T], where=at_uT)
        QK = sb("QK", [P, 6, T], where=w)
        VT = sb("VT", [P, 2, T], where=w)
        KC = sb("KC", [P, 2, T], where=w)
        mg = sb("mg", [P, 16, T], where=w)
        mark = w[0]
        cosT = sb("cosT", [P, N_STATE_TILES, T], where=w)
        sinT = sb("sinT", [P, N_STATE_TILES, T], where=w)
        sv = sb("sv", [P, 12, 16], where=w)
        CD = sb("CD", [P, 3, 16, 32], where=w)
        BT = sb("BT", [P, 2, 4, P], where=w)
        at_set = [w[0]]
        BC = sb("BC", [P, 4, 16, 16], where=w)
        BB = sb("BB", [P, 2, 16, 16], where=at_sq)
        BD = sb("BD", [P, 2, 16, 32], where=w)
        end_ssm = w[0]
        zin = sb("zin", [P, 2, T], where=at_set)
        pr1 = sb("pr1", [P, 2, 2 * T], where=at_ahi)
        pr2 = sb("pr2", [P, 2, 2 * T], where=at_ahi)
        t1 = sb("t1", [P, 2 * T], where=at_alo)
        t2 = sb("t2", [P, 2 * T], where=at_alo)
        zz = sb("zz", [P, 2, 2 * T], where=at_alo)
        at_ahi[0] -= 8 * 4 * T
        at_alo[0] -= 8 * 4 * T
        yg = sb("yg", [P, 4, T], where=at_ahi)
        sg = sb("sg", [P, 4, T], where=at_ahi)
        yghi = sb("yghi", [P, 4, T], F32R, where=at_alo)
        yglo = sb("yglo", [P, 4, T], F32R, where=at_alo)
        w = [mark]
        yshi = sb("yshi", [P, 4, T], F32R, where=w)
        yslo = sb("yslo", [P, 4, T], F32R, where=w)
        mrg = sb("mrg", [P, KT, T], where=w)
        alibi = sb("alibi", [P, NH, T], where=w)
        alibc = sb("alibc", [P, TT, NH, 16], where=w)
        maskc = sb("maskc", [P, TT, HG, 16], where=w)
        pe_kv = sb("pe_kv", [P, 2, CMP_BLOCK], where=w)
        cw2 = sb("cw2", [P, 2, DH], where=w)
        wg24 = sb("wg24", [P, KT, 24], where=w)
        CP = sb("CP", [P, 2, NG, T], where=w)
        CX = sb("CX", [P, 2, T], where=w)
        gate = sb("gate", [P, TT, 24], where=w)
        rq = sb("rq", [P, TT, HG, NG], where=w)
        sdk = sb("sdk", [P, 2, T], where=w)
        hid = sb("hid", [P, 4, 16], where=w)
        kcr = sb("kcr", [P, 4, 16], where=w)
        VV = sb("VV", [P, 2, TT, P], where=w)
        VC = sb("VC", [P, HG, P], where=w)
        PC = sb("PC", [P, 2, HG, 32], where=w)
        end_nsa = w[0]
        w = [phase]
        hhi = sb("hhi", [P, FF1_T, T], F32R, where=w)
        hlo = sb("hlo", [P, FF1_T, T], F32R, where=w)
        fa = sb("fa", [P, 2, 2 * T], where=w)
        fs = sb("fs", [P, 2, T], where=w)
        fh = sb("fh", [P, 2, 2 * T], where=w)
        end_ffn = w[0]
        w = [phase]
        rqT = sb("rqT", [P, RH, T], where=w)
        rkT = sb("rkT", [P, RH, T], where=w)
        rv = sb("rv", [P, TT, RH * P], where=w)
        rgT = sb("rgT", [P, RH, T], where=w)
        qmT = sb("qmT", [P, 2, T], where=w)
        rr = sb("rr", [P, 2, 2, T], where=w)
        pos_i = sb("pos_i", [P, T], mybir.dt.int32, where=w)
        ang = sb("ang", [P, 3, T], where=w)
        csR = sb("csR", [P, 2, T], where=w)
        mixf = sb("mixf", [P, KT, T], where=w)
        m0 = w[0]
        dpm = sb("dpm", [P, 2, 2 * T], where=w)
        dd = sb("dd", [P, 2, 2 * T], where=w)
        aa = sb("aa", [P, 2, 2 * T], where=w)
        end_ret = w[0]
        w = [m0]
        cqh = sb("cqh", [P, 3, T], where=w)
        sd3 = sb("sd3", [P, 2, T], where=w)
        w_uq = sb("w_uq", [P, 2, XH * 96], where=w)
        w_ukv = sb("w_ukv", [P, XH, 192], where=w)
        krT = sb("krT", [P, T], where=w)
        end_mla = w[0]
        pTs = sb("pTs", [P, 17, P], where=[max(end_nsa, end_ret, end_mla)])
        ends = (end_ssm, end_nsa + 17 * P * 4, end_ffn, end_ret + 17 * P * 4, end_mla + 17 * P * 4)
        assert max(ends) <= nc.sbuf_usable_end, (ends, nc.sbuf_usable_end)

        PS = [ctx.enter_context(nc.psum_tensor(f"ps{i}", [P, 512], F32)) for i in range(8)]

        def two(b):
            return PS[b][:, :].rearrange("p (c t) -> p c t", c=2)

        def over(ap2, n):
            return ap2.unsqueeze(1).to_broadcast([ap2.shape[0], n, ap2.shape[1]])

        subs, parts, exp_to, parts_out = attention_plan(QK, rq, alibi, alibc, maskc, gate, kcr, VV, VC, qmT, mkT, mv,
                                     rqT, rkT, rv, mixf, ynf, pTs)
        chunks_to = [s["chunk0"] for s in subs] + [subs[-1]["chunk0"] + len(subs[-1]["chunks"])]
        FILL = {1: AT["w_mg", 2], 2: AT["w_mg", 3], 3: AT["w_mg", 4], 4: AT["w_mg", 5], 6: AT["w_mg", 6],
                7: AT["w_mg", 7], 9: AT["w_mem", 0], 10: AT["w_mem", 1], 12: AT["w_mem", 2], 13: AT["w_mem", 3]}

        def done(n):
            if UNITS[n][3]:
                return S("unit_split_done"), SPLIT_BEFORE[n] + 1
            return S("unit_plain_done"), PLAIN_BEFORE[n] + 1

        def down(name):
            return name in ("w_dn", "w_fd")

        ffns = [("up", AT["w_up", 0], AT["w_dn", 0], 16, 32)]
        for l in range(2):
            for h in range(2):
                ffns.append(("gu", AT["w_gu", l * 44 + h * 22], AT["w_fd", l * 32 + h * 16], 22, 22))
        SMALL = dict(x=[(xT, "x")], vecs=[(vecs, "vecs"), (tabs, "tabs")], mem=[(yT, "mem")], bc=[(BC, "bc")],
                     nsa=[(alibi, "alibi"), (alibc, "alibc"), (maskc, "maskc"), (pe_kv, "pe_kv"), (cw2, "cw2"),
                          (wg24, "w_g24")],
                     ret=[(dpm, "dpm"), (pos_i, "pos")], mla=[(w_uq, "w_uq"), (w_ukv, "w_ukv"), (pos_i, "pos")])


        def rounds_of(eng, count, fn, ns=None, chain=None, per=0):
            fn(None, 0)
            fn(None, 1)
            rounds = (count - 4) // RAW
            with eng.Fori(0, rounds) as i:
                if chain:
                    chain.open(i, per)
                for j in range(RAW):
                    fn(i, 2 + j)
                if chain:
                    chain.close(rounds)
            if ns:
                ns[0] += RAW * rounds
            for u in range(2 + RAW * rounds, count):
                fn(None, u)

        LAT_JOBS = [("q", 0), ("q", 1), ("q", 2), ("kr", 0), ("k", 0), ("k", 1), ("k", 2),
                    ("v", 0), ("v", 1), ("v", 2), ("v", 3), ("rot", 0), ("rot", 1), ("rot", 2)]
        last_split = len(SPLITS)

        block = ctx.enter_context(nc.Block())

        @block.sync
        def _(sp):
            def load(n):
                name, chunk, cols, split = UNITS[n]
                if n >= RAW:
                    m = n - RAW
                    if UNITS[m][3]:
                        sp.wait_ge(S("w_lo"), SPLIT_BEFORE[m] + 1)
                    else:
                        sp.wait_ge(S("unit_plain_done"), PLAIN_BEFORE[m] + 1)
                sp.dma_start(raw[:, n % RAW, 0:cols], A[name][chunk]).then_inc(S(f"w_in{n % RAW}"), 16)

            def load_rounds(n0, count):
                name, chunk, cols, _s = UNITS[n0]
                for n in range(n0, n0 + RAW):
                    load(n)
                rounds = (count - RAW) // RAW
                with sp.Fori(0, rounds) as i:
                    for j in range(RAW):
                        n = n0 + RAW + j
                        sp.wait_ge(S("w_lo"), i * RAW + (SPLIT_BEFORE[n0 + j] + 1))
                        sp.dma_start(raw[:, n % RAW, 0:cols], A[name][i * RAW + (chunk + RAW + j)])\
                          .then_inc(S(f"w_in{n % RAW}"), 16)
                for n in range(n0 + RAW * (rounds + 1), n0 + count):
                    load(n)

            n = 0
            for kind, up, dn, nup, kt in ffns:
                while n < up:
                    load(n)
                    n += 1
                load_rounds(up, nup)
                load_rounds(dn, 16)
                n = dn + 16
            sp.wait_ge(S("x_final"), 1)
            sp.dma_start(out, xT[:]).then_inc(S("out"), 16)
            sp.wait_ge(S("out"), 16)

        @block.scalar
        def _(act):
            ns = [0]
            norms = [0]
            xgs = [0]
            chain = Chain(act, S("act_chain"))

            def hi(m, i, cols):
                n = SPLITS[m]
                act.wait_ge(S(f"w_in{n % RAW}"), at_round(16 * (n // RAW + 1), i, 16))
                if m >= SPL:
                    act.wait_ge(S("unit_split_done"), at_round(m - SPL + 1, i, RAW))
                for h in range(2):
                    c = slice(h * cols // 2, (h + 1) * cols // 2)
                    nc.scalar.activation(whi[:, m % SPL, c], raw[:, n % RAW, c], ACT.Copy).then_inc(S("w_hi"), 1)

            def ensure(m, n):
                while ns[0] <= m and ns[0] < last_split and SPLITS[ns[0]] <= n + RAW:
                    hi(ns[0], None, UNITS[SPLITS[ns[0]]][2])
                    ns[0] += 1

            def ahead(n):
                ensure(SPLIT_BEFORE[n] + (2 if UNITS[n][3] else 1), n)

            def split_acts():
                q = xgs[0]
                xgs[0] += 1
                for h in range(2):
                    act.wait_ge(S("xg"), 2 * q + h + 1)
                    nc.scalar.activation(ahi[:, 4 * h:4 * h + 4], xg[:, 4 * h:4 * h + 4], ACT.Copy).then_inc(S("ahi"), 1)

            def warm_root():
                chain(nc.scalar.activation(warm[:], V["eps"], ACT.Sqrt))

            def root(scale=1.0 / D):
                c = norms[0]
                norms[0] += 1
                act.wait_ge(S("sum_sq"), c + 1)
                nc.scalar.activation(sd[:], PS[7][:, 0:T + TT], ACT.Sqrt, bias=V["eps"], scale=scale)\
                  .then_inc(S("root"), 1)

            for key in ("x", "vecs", "bc", "mem"):
                for dst, name in SMALL[key]:
                    act.dma_start(dst[:], A[name]).then_inc(S("in_" + key), 16)
            act.wait_ge(S("in_vecs"), 32)
            ensure(1, 0)
            split_acts()
            nc.scalar.activation(sv[:, 0], V["log_dt"], ACT.Exp).then_inc(S("dt"), 1)
            act.wait_ge(S("ar_dt"), 1)
            nc.scalar.activation(sv[:, 1], sv[:, 2], ACT.Exp).then_inc(S("decay"), 1)
            ahead(AT["w_u", 0])
            root()
            for n in (AT["w_u", 1], AT["w_q", 0], AT["w_q", 1], AT["w_kv", 1], AT["w_kv", 2], AT["w_kv", 0]):
                ahead(n)
            act.wait_ge(S("turn"), 1)
            nc.scalar.activation(sinT[:], cosT[:], ACT.Sin, scale=TWO_PI_IN).then_inc(S("sin"), 1)
            act.wait_ge(S("turn"), 2)
            nc.scalar.activation(cosT[:], cosT[:], ACT.Sin, scale=-TWO_PI_IN, bias=V["half_pi"]).then_inc(S("sin"), 1)
            act.wait_ge(S("sum_sq"), 2)
            norms[0] += 1
            nc.scalar.activation(rm[:], PS[7][:, 0:T + TT], ACT.Sqrt, bias=V["eps"], scale=1.0 / D)\
              .then_inc(S("root"), 1)
            for c in range(8):
                act.wait_ge(S("evac"), GROUP[AT["w_mg", c]] + 1)
                nc.scalar.activation(mg[:, 2 * c:2 * c + 2], mg[:, 2 * c:2 * c + 2], ACT.Sigmoid).then_inc(S("mix_gate"), 1)
            act.wait_ge(S("yv"), 4)
            act.wait_ge(S("c_done"), 16)
            nc.scalar.activation(yg[:], uT[:], ACT.Gelu_apprx_tanh).then_inc(S("yg"), 1)
            act.wait_ge(S("yg"), 1)
            nc.scalar.activation(yghi[:], yg[:], ACT.Copy).then_inc(S("yg"), 1)
            for dst, name in SMALL["nsa"]:
                act.dma_start(dst[:], A[name]).then_inc(S("in_nsa"), 16)
            act.wait_ge(S("cx"), 1)
            for g, src, dst in ((0, slice(0, 64), slice(64, P)), (1, slice(64, P), slice(0, 64))):
                act.dma_start(CP[dst, :, g, 0:BLOCK_COLS], CX[src, :, 0:BLOCK_COLS]).then_inc(S("cp_moved"), 16)
            act.wait_ge(*done(AT["w_c1", 1]))
            nc.scalar.activation(hid[:, :, 0:N_CMP], PS[6][:, 0:64].rearrange("p (a b) -> p a b", a=4)[:, :, 0:N_CMP],
                                 ACT.Gelu_apprx_tanh).then_inc(S("hid"), 1)
            ensure(SPLIT_BEFORE[AT["w_glu", 0]] + 1, AT["w_c1", 1])
            for c in range(2):
                ahead(AT["w_glu", c])
                act.wait_ge(S("evac"), GROUP[AT["w_glu", c]] + 1)
                nc.scalar.activation(sg[:, 2 * c:2 * c + 2], sg[:, 2 * c:2 * c + 2], ACT.Sigmoid).then_inc(S("ssm_gate"), 1)
            act.wait_ge(S("ys"), 1)
            nc.scalar.activation(yshi[:], yg[:], ACT.Copy).then_inc(S("yshi"), 1)
            for c in range(4):
                ahead(AT["w_ps", c])
            act.wait_ge(S("qk_sums"), 1)
            nc.scalar.activation(rq[:], PS[2][:, 0:16].rearrange("p (a b c) -> p a b c", a=TT, b=HG), ACT.Sqrt,
                                 bias=V["eps"], scale=1.0 / DH).then_inc(S("qk_root"), 1)
            nc.scalar.activation(sdk[:], two(3), ACT.Sqrt, bias=V["eps"], scale=1.0 / DH).then_inc(S("qk_root"), 1)
            act.wait_ge(S("gate_logit"), 1)
            nc.scalar.activation(gate[:], gate[:], ACT.Sigmoid).then_inc(S("gate"), 1)
            act.wait_ge(S("kc_sums"), 1)
            nc.scalar.activation(kcr[:, 2, 0:N_CMP], PS[6][:, 96:96 + N_CMP], ACT.Sqrt, bias=V["eps"], scale=1.0 / DH)\
              .then_inc(S("kc_root"), 1)

            def attention(steps):
                todo = [k for what, k in steps if what == "sub"]

                def exps(s):
                    a = s["index"]
                    b = a % 2
                    act.wait_ge(S("att_max"), a + 1)
                    if a >= 2:
                        act.wait_ge(S("att_tr"), chunks_to[a - 1])
                    for h in range(s["nh"]):
                        dst = pP[:, b, h * s["nk"]:(h + 1) * s["nk"]]
                        src = sS[:, b, h * s["nk"]:(h + 1) * s["nk"]] if s["bias"] else \
                            PS[2 + h // 2][:, h % 2 * T:h % 2 * T + T]
                        nc.scalar.activation(dst, src, ACT.Exp, bias=amx[:, b, 0, h:h + 1], scale=s["scale"] or 1.0,
                                             accum_out=amx[:, b, 1, h:h + 1]).then_inc(S("att_exp"), 1)

                def copies(s):
                    if s["pv"] > 0:
                        act.wait_ge(S("att_pv"), s["pv"])
                    for c, tiles in enumerate(s["chunks"]):
                        k = s["chunk0"] + c
                        act.wait_ge(S("att_tr"), k + 1)
                        slot, n = s["base"] + 4 * c, len(tiles)
                        nc.scalar.activation(pTs[:, slot:slot + n, :],
                                             PS[4 + k % 2][:, 0:n * P].rearrange("p (a b) -> p a b", b=P), ACT.Copy)\
                          .then_inc(S("att_copy"), 1)

                exps(todo[0])
                for n, s in enumerate(todo):
                    if n + 1 < len(todo):
                        exps(todo[n + 1])
                    copies(s)

            attention(parts["nsa"])
            act.wait_ge(S("att_out"), parts_out["nsa"])
            nc.scalar.activation(yshi[:], ynf[:], ACT.Copy).then_inc(S("yshi"), 1)
            for c in range(4):
                ahead(AT["w_pn", c])

            def copy_halves(src, need):
                for h in range(2):
                    act.wait_ge(*need(h))
                    nc.scalar.activation(ahi[:, 4 * h:4 * h + 4], src[:, 4 * h:4 * h + 4], ACT.Copy)\
                      .then_inc(S("ahi"), 1)

            copy_halves(mrg, lambda h: (S("merged"), 4 * h + 4))
            for c in range(4):
                ahead(AT["w_out", c])

            def ffn(f):
                kind, up, dn, nup, kt = ffns[f]
                g0 = GROUP[up]
                h0 = sum(x[3] for x in ffns[:f])
                split_acts()

                def weights(n, i, cols):
                    if i is None:
                        ahead(n)
                    else:
                        hi(SPLIT_BEFORE[n] + SPL, i, cols)

                def hidden(i, u):
                    weights(up + u, i, UNIT)
                    if i is None and u == 0:
                        root()
                    b = u % 2
                    if kind == "gu":
                        act.wait_ge(S("evac"), at_round(g0 + u + 1, i, RAW))
                        nc.scalar.activation(fs[:, b], fa[:, b, 0:T], ACT.Silu).then_inc(S("silu"), 1)
                        act.wait_ge(S("hidden"), at_round(h0 + u + 1, i, RAW))
                        dst = hhi[:, at_round(u, i, RAW), :]
                        nc.scalar.activation(dst, fh[:, b, 0:T], ACT.Copy).then_inc(S("hid_hi"), 1)
                    else:
                        act.wait_ge(S("hidden"), at_round(h0 + u + 1, i, RAW))
                        dst = hhi[:, bass.ds(at_round(2 * u, i, 2 * RAW), 2), :]
                        nc.scalar.activation(dst, fh[:, b].rearrange("p (c t) -> p c t", c=2), ACT.Copy)\
                          .then_inc(S("hid_hi"), 1)

                rounds_of(act, nup, hidden, ns)
                if f:
                    warm_root()
                rounds_of(act, 16, lambda i, u: weights(dn + u, i, UNITS[dn][2]), ns)
                if f >= 1:
                    root()

            ffn(0)

            def retention():
                act.wait_ge(*done(ffns[1][2] + 15))
                for dst, name in SMALL["ret"]:
                    act.dma_start(dst[:], A[name]).then_inc(S("in_ret"), 16)
                split_acts()
                for c in range(13):
                    ahead(AT["w_ret", c])
                    if c == 0:
                        root()
                rope_tables()
                act.wait_ge(S("evac"), GROUP[AT["w_ret", 11]] + 1)
                nc.scalar.activation(rgT[:], rgT[:], ACT.Silu).then_inc(S("ret_gate"), 1)
                for h in range(RH):
                    act.wait_ge(S("ret_exponent"), h + 1)
                    nc.scalar.activation(dd[:, h % 2], dd[:, h % 2], ACT.Exp).then_inc(S("ret_decay"), 1)
                for j in range(3):
                    act.wait_ge(S("ln_sum"), j + 1)
                    nc.scalar.activation(xg[:, 2 * j:2 * j + 2], two((4, 5, 3)[j]), ACT.Sqrt, bias=V["eps"], scale=1.0 / P)\
                      .then_inc(S("ln_root"), 1)

            def rope_tables():
                k = rope_count[0]
                rope_count[0] += 1
                act.wait_ge(S("angle"), k + 1)
                nc.scalar.activation(csR[:, 1], ang[:, 0], ACT.Sin).then_inc(S("rope"), 1)
                nc.scalar.activation(csR[:, 0], ang[:, 1], ACT.Sin, scale=-1.0, bias=V["half_pi"]).then_inc(S("rope"), 1)

            rope_count = [0]

            def latent():
                act.wait_ge(*done(ffns[3][2] + 15))
                for dst, name in SMALL["mla"]:
                    act.dma_start(dst[:], A[name]).then_inc(S("in_mla"), 16)
                split_acts()
                for c in range(3):
                    ahead(AT["w_mla", c])
                    if c == 0:
                        root()
                rope_tables()
                act.wait_ge(S("lat_sums"), 1)
                for c in range(2):
                    nc.scalar.activation(sd3[:, c], PS[2 + c][:, 0:T], ACT.Sqrt, bias=V["eps"],
                                         scale=1.0 / (2 * P >> c)).then_inc(S("lat_root"), 1)
                attention(parts["mla"])

            for l in range(2):
                ffn(1 + 2 * l)
                (retention, latent)[l]()
                attention(parts[f"mem{l}"])
                warm_root()
                copy_halves(mixf, lambda h: (S("att_out"), parts_out[f"mem{l}"]))
                for c in range(4):
                    ahead(AT["w_o", 4 * l + c])
                root()
                ffn(2 + 2 * l)

        @block.vector
        def _(dve):
            ns, norms, acts = [0], [0], [0]
            chain = Chain(dve, S("dve_chain"))
            tt, ts, stt, cp = nc.vector.tensor_tensor, nc.vector.tensor_scalar, nc.vector.scalar_tensor_tensor, nc.vector.tensor_copy

            def lo(m, i, cols):
                n = SPLITS[m]
                for h in range(2):
                    c = slice(h * cols // 2, (h + 1) * cols // 2)
                    dve.wait_ge(S("w_hi"), at_round(2 * m + h + 1, i, 2 * RAW))
                    ins = tt(wlo[:, m % SPL, c], raw[:, n % RAW, c], whi[:, m % SPL, c].bitcast(F32), ALU.subtract)
                ins.then_inc(S("w_lo"), 1)

            def ensure(m, n):
                while ns[0] <= m and ns[0] < last_split and SPLITS[ns[0]] <= n + RAW:
                    lo(ns[0], None, UNITS[SPLITS[ns[0]]][2])
                    ns[0] += 1

            def ahead(n):
                ensure(SPLIT_BEFORE[n] + (2 if UNITS[n][3] else 1), n)

            def group(n):
                ahead(n)
                dve.wait_ge(*done(n))
                return two(GROUP[n] % 2)

            def split_acts():
                q = acts[0]
                acts[0] += 1
                for h in range(2):
                    s = slice(4 * h, 4 * h + 4)
                    dve.wait_ge(S("ahi"), 2 * q + h + 1)
                    tt(alo[:, s], xg[:, s], ahi[:, s].bitcast(F32), ALU.subtract).then_inc(S("alo"), 1)

            def scale_acts(gain):
                for k in range(KT):
                    ins = ts(xg[:, k], xT[:, k], gain[:, k:k + 1], None, ALU.mult)
                    if k % 4 == 3:
                        ins.then_inc(S("xg"), 1)

            def inverse_root(dst=None):
                c = norms[0]
                norms[0] += 1
                dve.wait_ge(S("root"), c + 1)
                src = sd if dst is None else dst
                chain(nc.vector.reciprocal((r if dst is None else dst)[:], src[:]))

            def scaled(dst, n, rows=slice(0, P)):
                tt(dst, group(n), over(r[:, 0:T], 2), ALU.mult).then_inc(S("evac"), 1)

            dve.wait_ge(S("in_vecs"), 32)
            chain(ts(half_g[:], V["ng"], 0.5, None, ALU.mult))
            dve.wait_ge(S("in_x"), 16)
            scale_acts(V["norm1"])
            ensure(0, 0)
            split_acts()
            ensure(1, 0)
            dve.wait_ge(S("dt"), 1)
            chain(tt(sv[:, 2], V["a_re"], sv[:, 0], ALU.mult))
            ts(sv[:, 2], sv[:, 2], 1.0, None, ALU.mult).then_inc(S("ar_dt"), 1)
            ahead(AT["w_u", 0])
            inverse_root()
            scaled(uT[:, 0:2], AT["w_u", 0])
            scaled(uT[:, 2:4], AT["w_u", 1])
            scaled(QK[:, 0:2], AT["w_q", 0])
            scaled(QK[:, 2:4], AT["w_q", 1])
            for b in range(2):
                bank = group(AT["w_kv", b + 1])
                tt(QK[:, 4 + b], bank[:, 0], r[:, 0:T], ALU.mult)
                tt(VT[:, b], bank[:, 1], r[:, 0:T], ALU.mult).then_inc(S("evac"), 1)
            scaled(KC[:], AT["w_kv", 0])

            chain(tt(sv[:, 3], V["a_im"], sv[:, 0], ALU.mult))
            chain(ts(sv[:, 3], sv[:, 3], float(1 / (2 * np.pi)), None, ALU.mult))
            chain(ts(sv[:, 4], sv[:, 3], MAGIC, MAGIC, ALU.add, ALU.subtract))
            chain(tt(sv[:, 3], sv[:, 3], sv[:, 4], ALU.subtract))
            for j in range(N_STATE_TILES):
                ins = ts(cosT[:, j], C["tok"], sv[:, 3, j:j + 1], None, ALU.mult)
            chain(ins)
            scaled(mg[:, 0:2], AT["w_mg", 0])
            chain(ts(sinT[:], cosT[:], MAGIC, MAGIC, ALU.add, ALU.subtract))
            tt(cosT[:], cosT[:], sinT[:], ALU.subtract).then_inc(S("turn"), 1)
            scaled(mg[:, 2:4], AT["w_mg", 1])
            dve.wait_ge(S("sin"), 1)
            dve.wait_ge(S("turn"), 1)
            stt(cosT[:], cosT[:], -1.0, cosT[:], ALU.mult, ALU.max).then_inc(S("turn"), 1)
            inverse_root(rm)
            chain(tt(yT[:], yT[:], over(rm[:, 0:T], KT), ALU.mult))
            for k in range(KT):
                ins = ts(yT[:, k], yT[:, k], V["memg"][:, k:k + 1], None, ALU.mult)
            ins.then_inc(S("mem_normed"), 1)
            dve.wait_ge(S("sin"), 2)
            dve.wait_ge(S("decay"), 1)
            tt(sv[:, 5], sv[:, 1], cosT[:, :, 1], ALU.mult)
            tt(sv[:, 6], sv[:, 1], sinT[:, :, 1], ALU.mult)
            tt(sv[:, 7], V["a_re"], V["a_re"], ALU.mult)
            chain(tt(sv[:, 8], V["a_im"], V["a_im"], ALU.mult))
            ts(sv[:, 5], sv[:, 5], -1.0, None, ALU.add)
            chain(tt(sv[:, 7], sv[:, 7], sv[:, 8], ALU.add))
            chain(nc.vector.reciprocal(sv[:, 7], sv[:, 7]))
            tt(sv[:, 8], sv[:, 5], V["a_re"], ALU.mult)
            tt(sv[:, 9], sv[:, 6], V["a_im"], ALU.mult)
            tt(sv[:, 10], sv[:, 6], V["a_re"], ALU.mult)
            chain(tt(sv[:, 11], sv[:, 5], V["a_im"], ALU.mult))
            tt(sv[:, 8], sv[:, 8], sv[:, 9], ALU.add)
            chain(tt(sv[:, 10], sv[:, 10], sv[:, 11], ALU.subtract))
            tt(sv[:, 8], sv[:, 8], sv[:, 7], ALU.mult)
            chain(tt(sv[:, 9], sv[:, 10], sv[:, 7], ALU.mult))
            dve.wait_ge(S("in_bc"), 16)
            dve.wait_ge(S("zeroed"), 1)

            def each_channel(v):
                return v.unsqueeze(2).to_broadcast([v.shape[0], 16, 16])

            for part, op in ((0, ALU.subtract), (1, ALU.add)):
                if part:
                    dve.wait_ge(S("bd"), 1)
                tt(BB[:, 0], BC[:, part], each_channel(sv[:, 8]), ALU.mult)
                chain(tt(BB[:, 1], BC[:, 1 - part], each_channel(sv[:, 9]), ALU.mult))
                for h in range(2):
                    rows = slice(64 * h, 64 * h + 64)
                    ins = tt(BD[rows, part, :, 16 * h:16 * h + 16], BB[rows, 0], BB[rows, 1], op)
                ins.then_inc(S("bd"), 1)
            for h in range(2):
                rows, cs = slice(64 * h, 64 * h + 64), slice(16 * h, 16 * h + 16)
                cp(CD[rows, 0, :, cs], BC[rows, 2])
                ts(CD[rows, 1, :, cs], BC[rows, 2], -1.0, None, ALU.mult)
                ins = ts(CD[rows, 2, :, cs], BC[rows, 3], -1.0, None, ALU.mult)
            ins.then_inc(S("cd"), 1)
            dve.wait_ge(S("bt_tr"), 1)
            for part in range(2):
                ins = cp(BT[:, part], PS[4 + part][:, :].rearrange("p (c s) -> p c s", c=4))
            ins.then_inc(S("bt"), 1)

            for j in range(N_STATE_TILES):
                b = j % 2
                dve.wait_ge(S("bu_done"), j + 1)
                bu = two(2 + b)
                tt(t1[:].rearrange("p (c t) -> p c t", c=2), bu, over(cosT[:, j], 2), ALU.mult)
                tt(t2[:].rearrange("p (c t) -> p c t", c=2), bu, over(sinT[:, j], 2), ALU.mult).then_inc(S("bu_read"), 1)
                dve.wait_ge(S("bu_read"), j + 1)
                tt(zin[:, 0], t1[:, 0:T], t2[:, T:2 * T], ALU.add)
                chain(tt(zin[:, 1], t1[:, T:2 * T], t2[:, 0:T], ALU.subtract))
                if j >= 2:
                    dve.wait_ge(S("turned"), 2 * (j - 1))
                for part in range(2):
                    nc.vector.tensor_tensor_scan(zz[:, b, part * T:part * T + T], sv[:, 1, j:j + 1].to_broadcast([P, T]),
                                                 zin[:, part], 0.0, ALU.mult, ALU.add).then_inc(S("scanned"), 1)
                if j in FILL:
                    n = FILL[j]
                    name, c = UNITS[n][:2]
                    if name == "w_mg":
                        scaled(mg[:, 2 * c:2 * c + 2], n)
                    else:
                        dst = mv[:, c // 2] if c % 2 else mkT[:, c // 2]
                        dve.wait_ge(*done(n))
                        cp(dst, two(GROUP[n] % 2)).then_inc(S("evac"), 1)
            for k in range(4):
                dve.wait_ge(S("c_done"), 8 * (k // 2 + 1))
                stt(uT[:, k], uT[:, k], V["d_skip"][:, k:k + 1], two(4 + k // 2)[:, k % 2], ALU.mult, ALU.add)\
                    .then_inc(S("yv"), 1)
            dve.wait_ge(S("yg"), 2)
            tt(yglo[:], yg[:], yghi[:].bitcast(F32), ALU.subtract).then_inc(S("yglo"), 1)
            dve.wait_ge(S("in_nsa"), 96)
            for kv in range(2):
                for g in range(NG):
                    rows = slice(DH * g, DH * g + DH)
                    for half in (1 - g, g):
                        dst = CP[rows, kv, g] if half == g else CX[rows, kv]
                        t0 = CMP_STRIDE * half
                        ins = tt(dst[:, 0:BLOCK_COLS].rearrange("p (c j) -> p c j", j=CMP_STRIDE),
                                 KC[rows, kv, t0:t0 + BLOCK_COLS].rearrange("p (c j) -> p c j", j=CMP_STRIDE),
                                 over(pe_kv[rows, kv, t0:t0 + CMP_STRIDE], N_CMP), ALU.add)
            ins.then_inc(S("cx"), 1)
            dve.wait_ge(S("vv_tr"), 1)
            cp(VV[:], PS[5][:, :].rearrange("p (a b c) -> p a b c", a=2, b=TT)).then_inc(S("vv"), 1)
            ensure(SPLIT_BEFORE[AT["w_glu", 0]] + 1, AT["w_c1", 1])
            for c in range(2):
                bank = group(AT["w_glu", c])
                for t in range(2):
                    k = 2 * c + t
                    ins = ts(sg[:, k], bank[:, t], V["b_glu"][:, k:k + 1], None, ALU.add)
                ins.then_inc(S("evac"), 1)
            dve.wait_ge(S("ssm_gate"), 2)
            tt(yg[:], yg[:], sg[:], ALU.mult).then_inc(S("ys"), 1)
            dve.wait_ge(S("yshi"), 1)
            tt(yslo[:], yg[:], yshi[:].bitcast(F32), ALU.subtract).then_inc(S("yslo"), 1)
            for c in range(4):
                bank = group(AT["w_ps", c])
                dve.wait_ge(S("mix_gate"), 8)
                tt(mrg[:, 2 * c:2 * c + 2], bank, mg[:, 2 * c:2 * c + 2], ALU.mult).then_inc(S("evac"), 1)
            dve.wait_ge(S("qk_root"), 2)
            nc.vector.reciprocal(rq[:], rq[:])
            chain(nc.vector.reciprocal(sdk[:], sdk[:]))
            chain(ts(half_q[:], V["qg"], float(DH ** -0.5), None, ALU.mult))
            dve.wait_ge(S("qk_squares"), 1)
            ts(QK[:, 0:4], QK[:, 0:4], half_q[:, 0:1], None, ALU.mult)
            for b in range(2):
                ins = stt(QK[:, 4 + b], QK[:, 4 + b], V["kg"][:, b + 1:b + 2], sdk[:, b], ALU.mult, ALU.mult)
            ins.then_inc(S("qk_ready"), 1)
            dve.wait_ge(S("gates_done"), 1)
            for t in range(TT):
                ins = ts(gate[:, t], PS[4][:, 32 + 24 * t:56 + 24 * t], r[:, T + t:T + t + 1], None, ALU.mult)
            ins.then_inc(S("gate_logit"), 1)
            dve.wait_ge(S("kvc_done"), 1)
            dve.wait_ge(S("nsa_zeroed"), 1)
            cp(kcr[:, 0, 0:N_CMP], PS[6][:, 64:64 + N_CMP]).then_inc(S("kc"), 1)
            for i in range(4):
                ins = cp(VC[32 * i:32 * i + N_CMP, i, :], PS[7][32 * i:32 * i + N_CMP, 64:64 + P])
            chain(ins)
            dve.wait_ge(S("kc_root"), 1)
            chain(nc.vector.reciprocal(kcr[:, 2, 0:N_CMP], kcr[:, 2, 0:N_CMP]))
            stt(kcr[:, 3, 0:N_CMP], kcr[:, 0, 0:N_CMP], V["kg"][:, 0:1], kcr[:, 2, 0:N_CMP], ALU.mult, ALU.mult)\
                .then_inc(S("kc_ready"), 1)
            dve.wait_ge(S("gate"), 1)

            def attention(steps, exps_before):
                subs_here = [k for what, k in steps if what == "sub"]

                def prep(s):
                    a, b, nh, nk = s["index"], s["index"] % 2, s["nh"], s["nk"]
                    dve.wait_ge(S("att_score"), a + 1)
                    if s["bias"]:
                        if a >= 2:
                            dve.wait_ge(S("att_exp"), exp_to[a - 1])
                        for h in range(nh):
                            src = PS[2 + h * s["hs"] // 512][:, h * s["hs"] % 512:h * s["hs"] % 512 + nk]
                            ins = stt(sS[:, b, h * nk:(h + 1) * nk], src, s["rowscale"][h], s["bias"][h],
                                      ALU.mult, ALU.add)
                        ins.then_inc(S("att_read"), 1)
                        dve.wait_ge(S("att_read"), s["read"])
                        src = sS[:, b, 0:nh * nk].rearrange("p (h k) -> p h k", h=nh)
                        chain(nc.vector.reduce_max(amx[:, b, 0, 0:nh], src, AX))
                    else:
                        for h in range(0, nh, 2):
                            m = min(2, nh - h)
                            ins = nc.vector.reduce_max(amx[:, b, 0, h:h + m], two(2 + h // 2)[:, 0:m], AX)
                        chain(ins)
                    ts(amx[:, b, 0, 0:nh], amx[:, b, 0, 0:nh], -(s["scale"] or 1.0), None, ALU.mult)\
                        .then_inc(S("att_max"), 1)

                def norm(s):
                    a, b, nh, nk = s["index"], s["index"] % 2, s["nh"], s["nk"]
                    dve.wait_ge(S("att_exp"), exp_to[a + 1])
                    chain(nc.vector.reciprocal(amx[:, b, 2, 0:nh], amx[:, b, 1, 0:nh]))
                    if s["gate"] is not None:
                        chain(tt(amx[:, b, 2, 0:nh], amx[:, b, 2, 0:nh], s["gate"], ALU.mult))
                    src = pP[:, b, 0:nh * nk].rearrange("p (h k) -> p h k", h=nh)
                    wgt = amx[:, b, 2, 0:nh].unsqueeze(2).to_broadcast([P, nh, nk])
                    if s["mask"] is not None:
                        chain(tt(src, src, s["mask"], ALU.mult))
                        c = s["cmp"]
                        if c >= 2:
                            dve.wait_ge(S("att_tr"), s["pc_free"])
                        tt(PC[:, c % 2, :, 0:nk], src, wgt, ALU.mult).then_inc(S("att_prob"), 1)
                    else:
                        tt(src, src, wgt, ALU.mult).then_inc(S("att_prob"), 1)

                def result(s):
                    dve.wait_ge(S("att_pv"), s["index"] + 1)
                    src = PS[6 + s["index"] % 2][s["rows"], 0:s["n"] * P].rearrange("p (a b) -> p a b", b=P)
                    cp(s["dest"], src).then_inc(S("att_out"), 1)

                prep(subs_here[0])
                k, late = 0, None
                for what, s in steps:
                    if what == "sub":
                        k += 1
                        if k < len(subs_here):
                            prep(subs_here[k])
                        norm(s)
                        if late is not None:
                            result(late)
                            late = None
                    else:
                        late = s
                result(late)

            attention(parts["nsa"], 0)
            dve.wait_ge(S("yshi"), 2)
            tt(yslo[:], ynf[:], yshi[:].bitcast(F32), ALU.subtract).then_inc(S("yslo"), 1)
            for c in range(4):
                s = slice(2 * c, 2 * c + 2)
                bank = group(AT["w_pn", c])
                tt(mg[:, 8 + 2 * c:10 + 2 * c], bank, mg[:, 8 + 2 * c:10 + 2 * c], ALU.mult).then_inc(S("evac"), 1)
                dve.wait_ge(S("evac"), GROUP[AT["w_pn", c]] + 1)
                for k in range(2 * c, 2 * c + 2):
                    tt(mrg[:, k], mrg[:, k], mg[:, 8 + k], ALU.add).then_inc(S("merged"), 1)

            def split_halves(src):
                q = acts[0]
                acts[0] += 1
                for h in range(2):
                    s = slice(4 * h, 4 * h + 4)
                    dve.wait_ge(S("ahi"), 2 * q + h + 1)
                    tt(alo[:, s], src[:, s], ahi[:, s].bitcast(F32), ALU.subtract).then_inc(S("alo"), 1)

            split_halves(mrg)
            for c in range(4):
                s = slice(2 * c, 2 * c + 2)
                tt(xT[:, s], group(AT["w_out", c]), xT[:, s], ALU.add).then_inc(S("evac"), 1)
            dve.wait_ge(S("evac"), GROUP[AT["w_out", 3]] + 1)
            scale_acts(V["norm2"])


            def post(gain, gain_next):
                inverse_root()
                for h in range(2):
                    s = slice(4 * h, 4 * h + 4)
                    chain(tt(yT[:, s], yT[:, s], over(r[:, 0:T], 4), ALU.mult))
                    for k in range(4 * h, 4 * h + 4):
                        ins = stt(xT[:, k], yT[:, k], gain[:, k:k + 1], xT[:, k], ALU.mult, ALU.add)
                    if gain_next is None and h:
                        ins.then_inc(S("x_final"), 1)
                        continue
                    chain(ins)
                    if gain_next is not None:
                        for k in range(4 * h, 4 * h + 4):
                            ins = ts(xg[:, k], xT[:, k], gain_next[:, k:k + 1], None, ALU.mult)
                        ins.then_inc(S("xg"), 1)

            def ffn(f):
                kind, up, dn, nup, kt = ffns[f]
                g0 = GROUP[up]
                h0 = sum(x[3] for x in ffns[:f])
                s0 = sum(x[3] for x in ffns[:f] if x[0] == "gu")
                split_acts()

                def weights(n, i, cols):
                    if i is None:
                        ahead(n)
                    else:
                        lo(SPLIT_BEFORE[n] + SPL, i, cols)

                def hidden(i, u):
                    if i is None and u == 0:
                        weights(up, i, UNIT)
                        inverse_root()
                    b = u % 2
                    sem, v = done(up + u)
                    dve.wait_ge(sem, at_round(v, i, RAW))
                    fab = fa[:, b].rearrange("p (c t) -> p c t", c=2)
                    tt(fab, two((g0 + u) % 2), over(r[:, 0:T], 2), ALU.mult).then_inc(S("evac"), 1)
                    if i is not None or u:
                        weights(up + u, i, UNIT)
                    if i is not None or u >= 2:
                        dve.wait_ge(S("hid_lo"), at_round(h0 + u - 1, i, RAW))
                    if kind == "gu":
                        dve.wait_ge(S("silu"), at_round(s0 + u + 1, i, RAW))
                        tt(fh[:, b, 0:T], fs[:, b], fa[:, b, T:2 * T], ALU.mult).then_inc(S("hidden"), 1)
                    else:
                        dve.wait_ge(S("evac"), at_round(g0 + u + 1, i, RAW))
                        stt(fh[:, b], fa[:, b], 0.0, fa[:, b], ALU.max, ALU.mult).then_inc(S("hidden"), 1)

                def result(i, u):
                    weights(dn + u, i, UNITS[dn][2])
                    if u % 2:
                        j = at_round(u // 2, i, 2)
                        sem, v = done(dn + u)
                        dve.wait_ge(sem, at_round(v, i, RAW))
                        src = PS[2 + u // 2 % 2][:, 0:T]
                        if kind == "gu":
                            cp(yT[:, j, :], src).then_inc(S("down_read"), 1)
                        else:
                            tt(xT[:, j, :], src, xT[:, j, :], ALU.add).then_inc(S("down_read"), 1)

                rounds_of(dve, nup, hidden, ns)
                rounds_of(dve, 16, result, ns)

            ffn(0)
            dve.wait_ge(S("down_read"), 8)
            scale_acts(V["ng"][:, 0:8])

            def rope_angle(inv):
                chain(cp(ang[:, 1], pos_i[:]))
                chain(ts(ang[:, 0], ang[:, 1], inv, None, ALU.mult))
                chain(ts(ang[:, 1], ang[:, 0], float(1 / (2 * np.pi)), None, ALU.mult))
                chain(ts(ang[:, 1], ang[:, 1], MAGIC, MAGIC, ALU.add, ALU.subtract))
                chain(stt(ang[:, 0], ang[:, 1], -C_HI, ang[:, 0], ALU.mult, ALU.add))
                chain(stt(ang[:, 0], ang[:, 1], -C_LO, ang[:, 0], ALU.mult, ALU.add))
                chain(ts(ang[:, 0], ang[:, 0], 3.1415925, -3.1415925, ALU.min, ALU.max))
                stt(ang[:, 1], ang[:, 0], -1.0, ang[:, 0], ALU.mult, ALU.max).then_inc(S("angle"), 1)

            def turn(dst, bank, rows, cnt, k):
                if k:
                    dve.wait_ge(S("rotated"), k)
                tt(rr[rows, 1], bank, over(csR[rows, 1], 2), ALU.mult).then_inc(S("rot_read"), 1)
                dve.wait_ge(S("rot_read"), k + 1)
                dve.wait_ge(S("rot_cos"), k + 1)
                tt(dst, rr[rows, 0], rr[rows, 1], ALU.add).then_inc(S("rotated"), 1)

            def retention():
                split_acts()
                u0 = AT["w_ret", 0]
                ahead(u0)
                inverse_root()
                for c in range(3):
                    scaled(rqT[:, 2 * c:2 * c + 2], u0 + c)
                for c in range(3):
                    scaled(rkT[:, 2 * c:2 * c + 2], u0 + 3 + c)
                for c in range(3):
                    bank = group(u0 + 6 + c)
                    for t in range(TT):
                        ins = ts(rv[:, t, 256 * c:256 * c + 256], bank[:, t], r[:, T + t:T + t + 1], None, ALU.mult)
                    ins.then_inc(S("evac"), 1)
                for c in range(3):
                    scaled(rgT[:, 2 * c:2 * c + 2], u0 + 9 + c)
                scaled(qmT[:], u0 + 12)
                dve.wait_ge(S("in_ret"), 32)
                rope_angle(V["inv_ret"])
                dve.wait_ge(S("rope"), 2)
                for k in range(6):
                    dve.wait_ge(S("rot_done"), k + 1)
                    dst = (rqT, rkT)[k // 3][:, 2 * (k % 3):2 * (k % 3) + 2]
                    turn(dst, two(2 + k % 2), slice(0, P), 2, k)
                for h in range(RH):
                    b = h % 2
                    dve.wait_ge(S("ret_forward"), h + 1)
                    stt(dd[:, b], dpm[:, 1], V["lg_b"][:, h:h + 1], dd[:, b], ALU.mult, ALU.add).then_inc(S("ret_exponent"), 1)
                    dve.wait_ge(S("ret_decay"), h + 1)
                    dve.wait_ge(S("ret_score"), h + 1)
                    stt(aa[:, b], PS[2 + b][:, :], float(P ** -0.5), dd[:, b], ALU.mult, ALU.mult).then_inc(S("ret_weight"), 1)
                    dve.wait_ge(S("ret_value"), h + 1)
                    cp(mixf[:, h], PS[4 + b][:, 0:T]).then_inc(S("ret_out"), 1)
                for j in range(3):
                    dve.wait_ge(S("ln_mean"), j + 1)
                    s = slice(2 * j, 2 * j + 2)
                    stt(mixf[:, s], two((6, 7, 2)[j]), -1.0 / P, mixf[:, s], ALU.mult, ALU.add).then_inc(S("centred"), 1)
                for j in range(3):
                    s = slice(2 * j, 2 * j + 2)
                    dve.wait_ge(S("ln_root"), j + 1)
                    chain(nc.vector.reciprocal(xg[:, s], xg[:, s]))
                    for h in range(2 * j, 2 * j + 2):
                        ins = stt(mixf[:, h], mixf[:, h], V["head_norm"][:, h:h + 1], xg[:, h], ALU.mult, ALU.mult)
                    chain(ins)
                    dve.wait_ge(S("ret_gate"), 1)
                    chain(tt(mixf[:, s], mixf[:, s], rgT[:, s], ALU.mult))

            def latent():
                split_acts()
                u0 = AT["w_mla", 0]
                ahead(u0)
                inverse_root()
                scaled(cqh[:, 0:2], u0)
                bank = group(u0 + 1)
                tt(cqh[:, 2], bank[:, 0], r[:, 0:T], ALU.mult)
                tt(krT[64:96], bank[64:96, 1], r[64:96, 0:T], ALU.mult).then_inc(S("evac"), 1)
                scaled(qmT[:], u0 + 2)
                dve.wait_ge(S("in_mla"), 48)
                rope_angle(V["inv_mla"])
                dve.wait_ge(S("lat_root"), 2)
                chain(nc.vector.reciprocal(sd3[:], sd3[:]))
                dve.wait_ge(S("lat_squares"), 1)
                for k in range(3):
                    g = V["cq_g"][:, k:k + 1] if k < 2 else V["ckv_g"]
                    ins = stt(cqh[:, k], cqh[:, k], g, sd3[:, k // 2], ALU.mult, ALU.mult)
                ins.then_inc(S("lat_ready"), 1)
                dve.wait_ge(S("rope"), 4)
                for t, (what, j) in enumerate(LAT_JOBS):
                    dve.wait_ge(S("lat_done"), t + 1)
                    b = 2 + t % 6
                    if what == "q":
                        cp(rqT[0:96, 2 * j:2 * j + 2], two(b)[0:96]).then_inc(S("lat_read"), 1)
                    elif what == "k":
                        cp(rkT[0:64, 2 * j:2 * j + 2], two(b)[0:64]).then_inc(S("lat_read"), 1)
                    elif what == "v":
                        cp(rv[:, j // 2, 384 * (j % 2):384 * (j % 2) + 384], PS[b][:, 0:384]).then_inc(S("lat_read"), 1)
                    elif what == "kr":
                        rows = slice(64, 96)
                        tt(rr[rows, 1, 0], PS[b][rows, 0:T], csR[rows, 1], ALU.mult).then_inc(S("lat_read"), 1)
                        dve.wait_ge(S("lat_read"), t + 1)
                        dve.wait_ge(S("kr_cos"), 1)
                        chain(tt(krT[rows], ang[rows, 2], rr[rows, 1, 0], ALU.add))
                        chain(cp(rkT[rows, :], over(krT[rows], XH)))
                    else:
                        rows = slice(0, 96)
                        dve.wait_ge(S("rotated"), 6 + j)
                        tt(rr[rows, 1], two(b)[0:96], over(csR[rows, 1], 2), ALU.mult).then_inc(S("lat_read"), 1)
                        dve.wait_ge(S("lat_read"), t + 1)
                        dve.wait_ge(S("rot_cos"), 6 + j + 1)
                        tt(rqT[rows, 2 * j:2 * j + 2], rr[rows, 0], rr[rows, 1], ALU.add).then_inc(S("rotated"), 1)
                attention(parts["mla"], 0)

            for l in range(2):
                ng = V["ng"][:, 48 * l:48 * l + 48]
                hg = half_g[:, 48 * l:48 * l + 48]
                ffn(1 + 2 * l)
                post(hg[:, 8:16], ng[:, 16:24])
                (retention, latent)[l]()
                attention(parts[f"mem{l}"], 0)
                split_halves(mixf)
                for c in range(4):
                    cp(yT[:, 2 * c:2 * c + 2], group(AT["w_o", 4 * l + c])).then_inc(S("evac"), 1)
                post(ng[:, 24:32], ng[:, 32:40])
                ffn(2 + 2 * l)
                post(hg[:, 40:48], None if l else V["ng"][:, 48:56])

        @block.gpsimd
        def _(pool):
            chain = Chain(pool, S("pool_chain"))
            sums, xgs = [0], [0]
            tt, ts = nc.gpsimd.tensor_tensor, nc.gpsimd.tensor_scalar

            def acc_free():
                c = sums[0]
                sums[0] += 1
                if c:
                    pool.wait_ge(S("sum_sq"), c)

            def squares(src, need):
                acc_free()
                for j in range(4):
                    s = slice(2 * j, 2 * j + 2)
                    pool.wait_ge(*need(j))
                    if j == 0:
                        chain(tt(acc2[:], src[:, s], src[:, s], ALU.mult))
                    else:
                        chain(tt(sq[:], src[:, s], src[:, s], ALU.mult))
                        chain(tt(acc2[:], acc2[:], sq[:], ALU.add))
                tt(acc[:], acc2[:, 0], acc2[:, 1], ALU.add).then_inc(S("acc"), 1)

            def squares_x():
                q = xgs[0]
                xgs[0] += 1
                squares(xT, lambda j: (S("xg"), 2 * q + 1 + j // 2))

            def squares_y(u, i, wait, first, last):
                j = at_round(u, i, 2)
                pool.wait_ge(*wait)
                if first:
                    acc_free()
                    chain(tt(acc[:], yT[:, j, :], yT[:, j, :], ALU.mult))
                    return
                chain(tt(sq[:, 0], yT[:, j, :], yT[:, j, :], ALU.mult))
                ins = tt(acc[:], acc[:], sq[:, 0], ALU.add)
                if last:
                    ins.then_inc(S("acc"), 1)
                else:
                    chain(ins)

            nc.gpsimd.memset(BD[:], 0.0)
            nc.gpsimd.memset(CD[:], 0.0).then_inc(S("zeroed"), 1)
            squares_x()
            squares(yT, lambda j: (S("in_mem"), 16))
            pool.wait_ge(*done(AT["w_kv", 0]))
            for j in range(N_STATE_TILES):
                b = j % 2
                pool.wait_ge(S("scanned"), 2 * (j + 1))
                if j >= 2:
                    pool.wait_ge(S("c_done"), j - 1)
                z = zz[:, b].rearrange("p (c t) -> p c t", c=2)
                tt(pr1[:, b].rearrange("p (c t) -> p c t", c=2), z, over(cosT[:, j], 2), ALU.mult).then_inc(S("turned"), 1)
                tt(pr2[:, b].rearrange("p (c t) -> p c t", c=2), z, over(sinT[:, j], 2), ALU.mult).then_inc(S("turned"), 1)
            pool.wait_ge(S("evac"), GROUP[AT["w_mem", 3]] + 1)
            tt(yT[:, 0:6], QK[:], QK[:], ALU.mult).then_inc(S("qk_squares"), 1)
            pool.wait_ge(S("c_done"), N_STATE_TILES)
            nc.gpsimd.memset(VC[:], 0.0)
            nc.gpsimd.memset(PC[:], 0.0).then_inc(S("nsa_zeroed"), 1)
            pool.wait_ge(S("kc"), 1)
            tt(kcr[:, 1, 0:N_CMP], kcr[:, 0, 0:N_CMP], kcr[:, 0, 0:N_CMP], ALU.mult).then_inc(S("kc_sq"), 1)

            def ffn(f):
                kind, up, dn, nup, kt = ffns[f]
                h0 = sum(x[3] for x in ffns[:f])
                squares_x()

                def low(i, u):
                    b = u % 2
                    pool.wait_ge(S("hid_hi"), at_round(h0 + u + 1, i, RAW))
                    if kind == "gu":
                        at = at_round(u, i, RAW)
                        dst, src, high = hlo[:, at, :], fh[:, b, 0:T], hhi[:, at, :]
                    else:
                        at = bass.ds(at_round(2 * u, i, 2 * RAW), 2)
                        dst, src, high = hlo[:, at, :], fh[:, b].rearrange("p (c t) -> p c t", c=2), hhi[:, at, :]
                    tt(dst, src, high.bitcast(F32), ALU.subtract).then_inc(S("hid_lo"), 1)

                def result(i, u):
                    if u % 2:
                        squares_y(u // 2, i, (S("down_read"), at_round(8 * f + u // 2 + 1, i, 2)),
                                  i is None and u == 1, i is None and u == 15)

                rounds_of(pool, nup, low)
                if f:
                    rounds_of(pool, 16, result, None, chain, 4)

            ffn(0)

            def turned_cos(k, dst, src, cs):
                pool.wait_ge(S("rotated"), k) if k else None
                tt(dst, src, over(cs, 2), ALU.mult).then_inc(S("rot_cos"), 1)

            def retention():
                pool.wait_ge(S("rope"), 2)
                pool.wait_ge(S("evac"), GROUP[AT["w_ret", 5]] + 1)
                for k in range(6):
                    turned_cos(k, rr[:, 0], (rqT, rkT)[k // 3][:, 2 * (k % 3):2 * (k % 3) + 2], csR[:, 0])
                for h in range(RH):
                    if h >= 2:
                        pool.wait_ge(S("ret_weight"), h - 1)
                    ts(dd[:, h % 2], dpm[:, 0], V["lg_f"][:, h:h + 1], None, ALU.mult).then_inc(S("ret_forward"), 1)
                for j in range(3):
                    s = slice(2 * j, 2 * j + 2)
                    pool.wait_ge(S("centred"), j + 1)
                    tt(yT[:, s], mixf[:, s], mixf[:, s], ALU.mult).then_inc(S("ln_squares"), 1)

            def latent():
                pool.wait_ge(S("evac"), GROUP[AT["w_mla", 1]] + 1)
                tt(yT[:, 0:3], cqh[:], cqh[:], ALU.mult).then_inc(S("lat_squares"), 1)
                pool.wait_ge(S("rope"), 4)
                pool.wait_ge(S("lat_squares"), 1)
                rows = slice(64, 96)
                tt(ang[rows, 2], krT[rows], csR[rows, 0], ALU.mult).then_inc(S("kr_cos"), 1)
                pool.wait_ge(S("kr_cos"), 1)
                pool.wait_ge(S("lat_read"), 4)
                rows = slice(0, 96)
                for j in range(3):
                    turned_cos(6 + j, rr[rows, 0], rqT[rows, 2 * j:2 * j + 2], csR[rows, 0])

            for l in range(2):
                ffn(1 + 2 * l)
                squares_x()
                (retention, latent)[l]()
                for k in range(KT):
                    squares_y(k, None, (S("evac"), GROUP[AT["w_o", 4 * l + k // 2]] + 1), k == 0, k == KT - 1)
                ffn(2 + 2 * l)

        @block.tensor
        def _(pe):
            sums, acts = [0], [0]
            mm, transpose = nc.tensor.matmul, nc.tensor.transpose

            def products(outs, n, high, low, kt, i=None, tokens=False, k0=0, first=True, last=True, need=None):
                name, chunk, cols, split = UNITS[n]
                wide = cols // kt
                for c, dst in enumerate(outs):
                    for k in range(kt):
                        if need and c == 0:
                            need(k)
                        ws = slice(k * wide, (k + 1) * wide) if tokens else \
                            slice(k * wide + c * P, k * wide + c * P + P)
                        xs = slice(c * P, c * P + P) if tokens else slice(0, T)
                        if split:
                            pairs = [(whi[:, n_slot(n), ws], high[:, k0 + k, xs]), (whi[:, n_slot(n), ws], low[:, k0 + k, xs]),
                                     (wlo[:, n_slot(n), ws], high[:, k0 + k, xs])]
                        else:
                            pairs = [(raw[:, n % RAW, ws], high[:, k0 + k, xs])]
                        for p, (wgt, x) in enumerate(pairs):
                            lhsT, rhs = (x, wgt) if tokens else (wgt, x)
                            ins = mm(dst, lhsT, rhs, start=first and k == 0 and p == 0,
                                     stop=last and k == kt - 1 and p == len(pairs) - 1)
                ins.then_inc(S("unit_split_done" if split else "unit_plain_done"), 1)

            def n_slot(n):
                return SPLIT_BEFORE[n] % SPL

            def unit(n, high, low, kt, i=None, tokens=False, need=None):
                g = GROUP[n]
                if g >= 2:
                    pe.wait_ge(S("evac"), at_round(g - 1, i, RAW))
                if UNITS[n][3]:
                    pe.wait_ge(S("w_lo"), at_round(SPLIT_BEFORE[n] + 1, i, RAW))
                else:
                    pe.wait_ge(S(f"w_in{n % RAW}"), 16 * (n // RAW + 1))
                bank = two(g % 2)
                products([bank[:, 0], bank[:, 1]], n, high, low, kt, i, tokens, need=need)

            def acts_need():
                q = acts[0]
                acts[0] += 1
                return lambda k: pe.wait_ge(S("alo"), 2 * q + 1 + k // 4) if k % 4 == 0 else None

            def sum_squares():
                c = sums[0]
                sums[0] += 1
                pe.wait_ge(S("acc"), c + 1)
                if c:
                    pe.wait_ge(S("root"), c)
                mm(PS[7][:, 0:T], C["ones"], acc[:], start=True, stop=True)
                for t in range(TT):
                    ins = mm(PS[7][:, T + t:T + t + 1], acc[:, t * P:t * P + P], C["ones"][:, 0:1], start=True, stop=True)
                ins.then_inc(S("sum_sq"), 1)

            pe.wait_ge(S("in_vecs"), 32)
            unit(AT["w_u", 0], ahi, alo, KT, need=acts_need())
            sum_squares()
            for n in (AT["w_u", 1], AT["w_q", 0], AT["w_q", 1], AT["w_kv", 1], AT["w_kv", 2], AT["w_kv", 0]):
                unit(n, ahi, alo, KT)
            sum_squares()
            unit(AT["w_mg", 0], xg, None, KT)
            unit(AT["w_mg", 1], xg, None, KT)
            for part in range(2):
                pe.wait_ge(S("bd"), part + 1)
                for c in range(4):
                    ins = transpose(PS[4 + part][:, c * P:c * P + P], BD[:, part, 4 * c:4 * c + 4, :], C["ident"])
            ins.then_inc(S("bt_tr"), 1)

            def inputs(j):
                b, rows = j % 2, slice(32 * (j % 4), 32 * (j % 4) + 32)
                if j >= 2:
                    pe.wait_ge(S("bu_read"), j - 1)
                for part in range(2):
                    ins = mm(two(2 + b)[:, part], BT[rows, part, j // 4, :], uT[rows, j // 4, :], start=True, stop=True)
                ins.then_inc(S("bu_done"), 1)

            def outputs(j):
                b, rows, q = j % 2, slice(32 * (j % 4), 32 * (j % 4) + 32), j // 4
                pe.wait_ge(S("turned"), 2 * (j + 1))
                dst = two(4 + q // 2)[rows, q % 2]
                terms = [(0, pr1[:, b, 0:T]), (1, pr2[:, b, T:2 * T]), (2, pr1[:, b, T:2 * T]), (2, pr2[:, b, 0:T])]
                for k, (c, x) in enumerate(terms):
                    ins = mm(dst, CD[:, c, j, :], x, start=k == 0, stop=k == 3)
                ins.then_inc(S("c_done"), 1)

            pe.wait_ge(S("bt"), 1)
            pe.wait_ge(S("cd"), 1)
            inputs(0)
            for j in range(N_STATE_TILES):
                if j + 1 < N_STATE_TILES:
                    inputs(j + 1)
                if j in FILL:
                    n = FILL[j]
                    if UNITS[n][0] == "w_mg":
                        unit(n, xg, None, KT)
                    else:
                        pe.wait_ge(S("mem_normed"), 1)
                        unit(n, yT, None, KT, tokens=bool(UNITS[n][1] % 2))
                outputs(j)
            pe.wait_ge(S("yv"), 4)
            for b in range(2):
                for t in range(TT):
                    ins = transpose(PS[5][:, (2 * b + t) * P:(2 * b + t + 1) * P], VT[:, b, t * P:t * P + P], C["ident"])
            ins.then_inc(S("vv_tr"), 1)
            pe.wait_ge(S("cx"), 1)
            pe.wait_ge(S("cp_moved"), 32)
            for kv in range(2):
                n = AT["w_c1", kv]
                pe.wait_ge(S(f"w_in{n % RAW}"), 16 * (n // RAW + 1))
                for j in range(CMP_STRIDE):
                    ins = mm(PS[6][:, 32 * kv:32 * kv + 32].rearrange("p (g c) -> p g c", g=NG)[:, :, 0:N_CMP],
                             raw[:, n % RAW, j * P:j * P + P], CP[:, kv, :, j:j + CMP_STRIDE * (N_CMP - 1) + 1:CMP_STRIDE],
                             start=j == 0, stop=j == CMP_STRIDE - 1)
                ins.then_inc(S("unit_plain_done"), 1)
            pe.wait_ge(S("yglo"), 1)
            for c in range(2):
                unit(AT["w_glu", c], yghi, yglo, GLU_KT)
            pe.wait_ge(S("qk_squares"), 1)
            for t in range(TT):
                for h in range(HG):
                    mm(PS[2][:, 8 * t + 2 * h:8 * t + 2 * h + 2], yT[:, h, t * P:t * P + P], C["gsel"], start=True, stop=True)
            mm(PS[3][:, :], C["bones"], yT[:, 4:6, :], start=True, stop=True).then_inc(S("qk_sums"), 1)
            for t in range(TT):
                for k in range(KT):
                    ins = mm(PS[4][:, 32 + 24 * t:56 + 24 * t], xg[:, k, t * P:t * P + P], wg24[:, k, :],
                             start=k == 0, stop=k == KT - 1)
            ins.then_inc(S("gates_done"), 1)
            pe.wait_ge(S("hid"), 1)
            for g in range(NG):
                mm(PS[6][g * DH:g * DH + DH, 64:64 + N_CMP], cw2[:, 0], hid[:, g, 0:N_CMP], start=True, stop=True)
            for i in range(4):
                for g in range(NG):
                    ins = mm(PS[7][32 * i:32 * i + N_CMP, 64 + g * DH:128 + g * DH], hid[:, 2 + g, 0:N_CMP], cw2[:, 1],
                             start=True, stop=True)
            ins.then_inc(S("kvc_done"), 1)
            pe.wait_ge(S("yslo"), 1)
            for c in range(4):
                unit(AT["w_ps", c], yshi, yslo, GLU_KT)
            pe.wait_ge(S("kc_sq"), 1)
            mm(PS[6][:, 96:96 + N_CMP], C["bones"], kcr[:, 1, 0:N_CMP], start=True, stop=True).then_inc(S("kc_sums"), 1)

            def attention(steps):
                todo = [k for what, k in steps if what == "sub"]

                def scores(s):
                    a, nk, hs = s["index"], s["nk"], s["hs"]
                    if a:
                        before = subs[a - 1]
                        if before["bias"]:
                            pe.wait_ge(S("att_read"), before["read"])
                        else:
                            pe.wait_ge(S("att_exp"), exp_to[a])
                    for h in range(s["nh"]):
                        ins = mm(PS[2 + h * hs // 512][:, h * hs % 512:h * hs % 512 + nk], s["q"][h], s["k"][h],
                                 start=True, stop=True)
                    ins.then_inc(S("att_score"), 1)

                def transposes(s):
                    a, b = s["index"], s["index"] % 2
                    pe.wait_ge(S("att_prob"), a + 1)
                    for c, tiles in enumerate(s["chunks"]):
                        k = s["chunk0"] + c
                        if k >= 2:
                            pe.wait_ge(S("att_copy"), k - 1)
                        for i, tile in enumerate(tiles):
                            src = PC[:, s["cmp"] % 2] if tile is None else \
                                pP[:, b, tile[0] * s["nk"] + tile[1] * P:tile[0] * s["nk"] + tile[1] * P + P]
                            ins = transpose(PS[4 + k % 2][:, i * P:i * P + P], src, C["ident"])
                        ins.then_inc(S("att_tr"), 1)

                def values(v):
                    i = v["index"]
                    pe.wait_ge(S("att_copy"), v["copied"])
                    if i >= 2:
                        pe.wait_ge(S("att_out"), i - 1)
                    for rows, slot, terms in v["outs"]:
                        for k, (lhsT, rhs) in enumerate(terms):
                            ins = mm(PS[6 + i % 2][rows, slot * P:slot * P + P], lhsT, rhs, start=k == 0,
                                     stop=k == len(terms) - 1)
                    ins.then_inc(S("att_pv"), 1)

                scores(todo[0])
                scores(todo[1])
                k = 1
                for what, s in steps:
                    if what == "sub":
                        k += 1
                        if k < len(todo):
                            scores(todo[k])
                        transposes(s)
                    else:
                        values(s)

            pe.wait_ge(S("qk_ready"), 1)
            pe.wait_ge(S("kc_ready"), 1)
            attention(parts["nsa"])
            pe.wait_ge(S("yslo"), 2)
            for c in range(4):
                unit(AT["w_pn", c], yshi, yslo, GLU_KT)
            need = acts_need()
            for c in range(4):
                unit(AT["w_out", c], ahi, alo, KT, need=need if c == 0 else None)

            def ffn(f):
                kind, up, dn, nup, kt = ffns[f]
                need = acts_need()
                h0 = sum(x[3] for x in ffns[:f])

                def hidden(i, u):
                    unit(up + u, ahi, alo, KT, i, need=need if i is None and u == 0 else None)
                    if i is None and u == 0:
                        sum_squares()

                def result(i, u):
                    n, j = dn + u, u // 2
                    pe.wait_ge(S("w_lo"), at_round(SPLIT_BEFORE[n] + 1, i, RAW))
                    if i is None and u < 2:
                        pe.wait_ge(S("hid_lo"), h0 + (u + 1) * nup // 2)
                    if u % 2 == 0 and (f or i is not None or j >= 2):
                        pe.wait_ge(S("down_read"), at_round(8 * f + j - 1, i, 2))
                    products([PS[2 + j % 2][:, 0:T]], n, hhi, hlo, kt // 2, i, k0=u % 2 * kt // 2,
                             first=u % 2 == 0, last=u % 2 == 1)

                rounds_of(pe, nup, hidden)
                rounds_of(pe, 16, result)
                if f:
                    sum_squares()

            ffn(0)

            def retention():
                need = acts_need()
                for c in range(13):
                    unit(AT["w_ret", c], ahi, alo, KT, tokens=6 <= c < 9, need=need if c == 0 else None)
                    if c == 0:
                        sum_squares()
                pe.wait_ge(S("evac"), GROUP[AT["w_ret", 5]] + 1)
                for k in range(6):
                    if k >= 2:
                        pe.wait_ge(S("rot_read"), k - 1)
                    mm(PS[2 + k % 2][:, :], C["rot_ret"], (rqT, rkT)[k // 3][:, 2 * (k % 3):2 * (k % 3) + 2, :],
                       start=True, stop=True).then_inc(S("rot_done"), 1)

                def score(h):
                    b = h % 2
                    pe.wait_ge(S("rotated"), 6)
                    if h >= 2:
                        pe.wait_ge(S("ret_weight"), h - 1)
                    for s in range(TT):
                        ins = mm(two(2 + b)[:, s], rkT[:, h, s * P:s * P + P], rqT[:, h, :], start=True, stop=True)
                    ins.then_inc(S("ret_score"), 1)

                score(0)
                for h in range(RH):
                    b = h % 2
                    if h + 1 < RH:
                        score(h + 1)
                    pe.wait_ge(S("ret_weight"), h + 1)
                    if h >= 2:
                        pe.wait_ge(S("ret_out"), h - 1)
                    for s in range(TT):
                        ins = mm(PS[4 + b][:, 0:T], rv[:, s, h * P:h * P + P], aa[:, b, s * T:s * T + T],
                                 start=s == 0, stop=s == TT - 1)
                    ins.then_inc(S("ret_value"), 1)
                for j in range(3):
                    pe.wait_ge(S("ret_out"), 2 * j + 2)
                    mm(PS[(6, 7, 2)[j]][:, :], C["ones"], mixf[:, 2 * j:2 * j + 2, :], start=True, stop=True)\
                        .then_inc(S("ln_mean"), 1)
                for j in range(3):
                    pe.wait_ge(S("ln_squares"), j + 1)
                    if j == 0:
                        pe.wait_ge(S("ret_out"), RH)
                    mm(PS[(4, 5, 3)[j]][:, :], C["ones"], yT[:, 2 * j:2 * j + 2, :], start=True, stop=True)\
                        .then_inc(S("ln_sum"), 1)
                pe.wait_ge(S("ln_root"), 3)

            def latent():
                need = acts_need()
                for c in range(3):
                    unit(AT["w_mla", c], ahi, alo, KT, need=need if c == 0 else None)
                    if c == 0:
                        sum_squares()
                pe.wait_ge(S("lat_squares"), 1)
                for k in range(3):
                    ins = mm(PS[2 + k // 2][:, 0:T], C["ones"], yT[:, k, :], start=k != 1, stop=k != 0)
                ins.then_inc(S("lat_sums"), 1)
                pe.wait_ge(S("lat_ready"), 1)
                pe.wait_ge(S("in_mla"), 48)
                for t, (what, j) in enumerate(LAT_JOBS):
                    b = 2 + t % 6
                    if t >= 6:
                        pe.wait_ge(S("lat_read"), t - 5)
                    if what == "q":
                        for h in range(2):
                            for k in range(2):
                                c0 = (2 * j + h) * 96
                                ins = mm(two(b)[0:96, h], w_uq[:, k, c0:c0 + 96], cqh[:, k, :], start=k == 0, stop=k == 1)
                    elif what == "kr":
                        ins = mm(PS[b][64:96, 0:T], C["rot_mla"][64:96, 64:96], krT[64:96, :], start=True, stop=True)
                    elif what == "k":
                        for h in range(2):
                            ins = mm(two(b)[0:64, h], w_ukv[:, 2 * j + h, 0:64], cqh[:, 2, :], start=True, stop=True)
                    elif what == "v":
                        c = j % 2
                        ins = mm(PS[b][:, 0:384], cqh[:, 2, j // 2 * P:j // 2 * P + P], w_ukv[:, 3 * c:3 * c + 3, 64:192],
                                 start=True, stop=True)
                    else:
                        ins = mm(PS[b][0:96, :], C["rot_mla"][0:96, 0:96], rqT[0:96, 2 * j:2 * j + 2, :], start=True, stop=True)
                    ins.then_inc(S("lat_done"), 1)
                pe.wait_ge(S("rotated"), 9)
                attention(parts["mla"])

            for l in range(2):
                ffn(1 + 2 * l)
                (retention, latent)[l]()
                pe.wait_ge(S("evac"), GROUP[AT[("w_ret", 12) if l == 0 else ("w_mla", 2)]] + 1)
                attention(parts[f"mem{l}"])
                need = acts_need()
                for c in range(4):
                    unit(AT["w_o", 4 * l + c], ahi, alo, KT, need=need if c == 0 else None)
                sum_squares()
                ffn(2 + 2 * l)


def chunked(w, nt):
    k, n = w.shape
    return w.reshape(k // P, P, n // (nt * P), nt * P).transpose(2, 1, 0, 3).reshape(n // (nt * P), P, -1)


def cols(v, n):
    return v.reshape(n, P).T


def layout(a):
    A = {}
    w_in = a["w_in"][0]
    o1, o2, o3, o4 = SSM_W, SSM_W + 512, SSM_W + 512 + 768, SSM_W + 512 + 768 + 24
    A["w_u"] = chunked(w_in[:, :o1], 2)
    q = w_in[:, o1:o2].reshape(D, NG, HG, DH).transpose(0, 2, 1, 3).reshape(D, 512)
    A["w_q"] = chunked(q, 2)
    A["w_kv"] = chunked(w_in[:, o2:o3], 2)
    A["w_g24"] = w_in[:, o3:o4].reshape(KT, P, 24).transpose(1, 0, 2)
    A["w_mg"] = chunked(w_in[:, o4:], 2)
    A["w_mem"] = np.concatenate([chunked(a["mem_w_kv_2"][l], 2) for l in range(2)])
    c1 = np.stack([a["cmp_wk1"][0], a["cmp_wv1"][0]]).reshape(2, 2, 16, DH, P).transpose(0, 1, 3, 2, 4)
    A["w_c1"] = c1.reshape(2, P, 16 * P)
    A["w_glu"] = chunked(a["ssm_w_glu"][0], 2)
    A["w_ps"] = chunked(a["w_proj_ssm"][0], 2)
    pn = a["w_proj_nsa"][0].reshape(NG, HG, DH, D).transpose(1, 0, 2, 3).reshape(512, D)
    A["w_pn"] = chunked(pn, 2)
    A["w_out"] = chunked(a["w_out"][0], 2)
    A["w_up"] = chunked(a["w_up"][0], 2)

    def halves(w):
        kt = w.shape[0] // P
        return w.reshape(2, kt // 2, P, KT, P).transpose(3, 0, 2, 1, 4).reshape(16, P, kt // 2 * P)
    A["w_dn"] = halves(a["w_down"][0])
    gu = a["ffn_w_gu_2"].reshape(4, KT, P, 2, FF2_T, P).transpose(0, 4, 2, 1, 3, 5)
    A["w_gu"] = gu.reshape(4 * FF2_T, P, UNIT)
    A["w_fd"] = np.concatenate([halves(a["ffn_w_down_2"][l, h]) for l in range(2) for h in range(2)])
    A["w_ret"] = chunked(a["ret_w_in_2"][0], 2)
    m = a["mla_w_in_2"][0]
    A["w_mla"] = chunked(np.concatenate([m[:, 0:384], m[:, 320:448], m[:, 416:672]], axis=1), 2)
    A["w_o"] = np.concatenate([chunked(a["w_o_2"][l], 2) for l in range(2)])
    A["w_uq"] = a["mla_w_uq_2"][0].reshape(2, P, XH * 96).transpose(1, 0, 2)
    A["w_ukv"] = a["mla_w_ukv_2"][0].reshape(P, XH, 192)
    A["x"] = a["x"][0].reshape(T, KT, P).transpose(2, 1, 0)
    A["mem"] = a["mem_2"][0].reshape(T, KT, P).transpose(2, 1, 0)
    A["pos"] = np.broadcast_to(a["positions_2"], (P, T))

    def state(v):
        return v.reshape(16, 2 * 64).T
    b = [v[0].reshape(16, P, 16).transpose(1, 0, 2) for v in (a["ssm_b_re"], a["ssm_b_im"])]
    c = [v[0].transpose(0, 2, 1).reshape(16, P, 16).transpose(1, 0, 2) for v in (a["ssm_c_re"], a["ssm_c_im"])]
    A["bc"] = np.stack(b + c, axis=1)
    f = np.float32
    inv_ret = (1.0 / (f(10000.0) ** (np.arange(0, 128, 2, dtype=f) / f(128)))).astype(f)
    inv_mla = (1.0 / (f(10000.0) ** (np.arange(0, ROPE, 2, dtype=f) / f(ROPE)))).astype(f)
    const = {"inv_ret": np.tile(inv_ret, 2), "inv_mla": np.concatenate([np.zeros(64, f), inv_mla, inv_mla, np.zeros(32, f)]),
             "half_pi": np.full(P, np.pi / 2, f), "eps": np.full(P, EPS, f)}
    v = {"norm1": cols(a["norm1_g"][0], 8), "norm2": cols(a["norm2_g"][0], 8),
         "ng": a["norm_gains_2"].reshape(96, P).T, "memg": cols(a["mem_norm_2"], 8),
         "a_re": state(a["ssm_a_re"][0]), "a_im": state(a["ssm_a_im"][0]),
         "log_dt": state(np.broadcast_to(a["ssm_log_dt"][0][:, None], (32, 64))),
         "d_skip": cols(a["ssm_d"][0], 4), "b_glu": cols(a["ssm_b_glu"][0], 4),
         "qg": np.tile(a["q_norm_g"][0], 2)[:, None], "kg": np.tile(a["k_norm_g"][0].T, (2, 1)),
         "head_norm": a["ret_head_norm_2"][0].T, "cq_g": cols(a["mla_q_norm_2"][0], 2), "ckv_g": cols(a["mla_kv_norm_2"][0], 1),
         "lg_f": np.broadcast_to(a["ret_log_decay_2"][0, 0], (P, 6)), "lg_b": np.broadcast_to(a["ret_log_decay_2"][0, 1], (P, 6))}
    A["vecs"] = np.concatenate([v[n] if n in v else const[n][:, None] for n, _ in VECS], axis=1)
    A["pe_kv"] = np.tile(np.stack([a["cmp_pe_k"][0].T, a["cmp_pe_v"][0].T], axis=1), (2, 1, 1))
    A["cw2"] = np.stack([a["cmp_wk2"][0], a["cmp_wv2"][0]], axis=1)
    i = np.arange(P)
    ident = np.eye(P, dtype=f)
    rot_ret = np.zeros((P, P), f)
    rot_ret[64 + np.arange(64), np.arange(64)] = -1.0
    rot_ret[np.arange(64), 64 + np.arange(64)] = 1.0
    rot_mla = np.zeros((P, P), f)
    rot_mla[80 + np.arange(16), 64 + np.arange(16)] = -1.0
    rot_mla[64 + np.arange(16), 80 + np.arange(16)] = 1.0
    t = {"ident": ident, "ones": np.ones((P, P), f), "bones": (i[:, None] // 64 == i[None] // 64).astype(f),
         "gsel": (i[:, None] // 64 == np.arange(2)[None]).astype(f), "rot_ret": rot_ret, "rot_mla": rot_mla,
         "tok": np.broadcast_to(np.arange(T, dtype=f), (P, T))}
    A["tabs"] = np.concatenate([t[n] for n, _ in TABS], axis=1)
    slopes = np.exp2(-8.0 * np.arange(1, NH + 1) / NH).astype(f)
    dist = (P + i[:, None] - np.arange(T)[None]).astype(f)
    A["alibi"] = np.where(dist[:, None] >= 0, -slopes[None, :, None] * dist[:, None], f(NEG)).astype(f)
    c_end = np.arange(16) * CMP_STRIDE + CMP_BLOCK - 1
    dc = ((np.arange(TT) * P)[None, :, None] + i[:, None, None] - c_end[None, None]).astype(f)
    ok = (dc >= 0) & (np.arange(16) < N_CMP)
    A["alibc"] = np.where(ok[:, :, None], -slopes[None, None, :, None] * dc[:, :, None], f(NEG)).astype(f)
    A["maskc"] = np.broadcast_to(ok[:, :, None], (P, TT, HG, 16)).astype(f)
    ts_ = np.arange(T)[None, None] - (np.arange(TT) * P)[None, :, None] - i[:, None, None]
    A["dpm"] = np.stack([np.maximum(ts_, 0), np.maximum(-ts_, 0)], axis=1).astype(f).reshape(P, 2, 2 * T)
    return {n: np.ascontiguousarray(v) for n, v in A.items()}


def kernel(**inputs):
    import concourse.bacc as bacc
    from concourse import mybir
    from concourse.bass_utils import run_bass_kernel_spmd
    arrays = layout({n: np.asarray(v) for n, v in inputs.items()})
    nc = bacc.Bacc("TRN2", target_bir_lowering=False, num_devices=1)
    A = {n: nc.dram_tensor("in_" + n, v.shape, mybir.dt.from_np(v.dtype), kind="ExternalInput").ap() for n, v in arrays.items()}
    out = nc.dram_tensor("out", (P, KT, T), mybir.dt.float32, kind="ExternalOutput").ap()
    program(nc, A, out)
    r = run_bass_kernel_spmd(nc, [{"in_" + n: v for n, v in arrays.items()}], core_ids=[0])
    return r.results[0]["out"].transpose(2, 1, 0).reshape(1, T, D)
```
